# Optimizing a Trainium2 kernel written in Bass

```python
import math
import jax, jax.numpy as jnp
from jax import lax
import numpy as np

D_MODEL = 1024
BATCH = 1
SEQ = 1024
DEPTH = 1
DEC_BATCH = 1
DEC_SEQ = 64
PAST_LEN = 1024

CHUNK = 64
Q_BLOCK = 128
H_A = 8
DH_A = 64
H_B = 4
DH_B = 64
DV_B = 2 * DH_B
W_A = H_A * DH_A
W_B = H_B * DV_B
D_FF = 2816
CONV_W = 3
EPS = 1e-6
LAYER_IDX = 1
LAMBDA_INIT = 0.8 - 0.6 * math.exp(-0.3 * (LAYER_IDX - 1))
ALIBI_SLOPES = np.array([2.0 ** (-8.0 * (i + 1) / H_B) for i in range(H_B)], dtype=np.float32)
SPLIT_POINTS = [W_A, 2 * W_A, 3 * W_A, 3 * W_A + H_A,
                3 * W_A + H_A + W_B, 3 * W_A + H_A + 2 * W_B, 3 * W_A + H_A + 3 * W_B,
                3 * W_A + H_A + 3 * W_B + D_MODEL]
N_IN = 3 * W_A + H_A + 3 * W_B + 2 * D_MODEL

kernel_name = 'hybrid_fox_diff_convffn_stream_step'

def rms_norm(x, g):
    xf = x.astype(jnp.float32)
    y = xf * lax.rsqrt(jnp.mean(xf * xf, axis=-1, keepdims=True) + EPS)
    return (y * g.astype(jnp.float32)).astype(x.dtype)

def mixer_inputs(x, g_attn, w_in, b_f, qn_a, kn_a, qn_b, kn_b):
    B, T, _ = x.shape
    z = rms_norm(x, g_attn) @ w_in
    qa, ka, va, fa, qb, kb, vb, gate_a, gate_b = jnp.split(z, SPLIT_POINTS, axis=-1)
    qa = rms_norm(qa.reshape(B, T, H_A, DH_A), qn_a)
    ka = rms_norm(ka.reshape(B, T, H_A, DH_A), kn_a)
    va = va.reshape(B, T, H_A, DH_A)
    logf = jax.nn.log_sigmoid((fa + b_f).astype(jnp.float32))
    qb = rms_norm(qb.reshape(B, T, H_B, 2, DH_B), qn_b)
    kb = rms_norm(kb.reshape(B, T, H_B, 2, DH_B), kn_b)
    vb = vb.reshape(B, T, H_B, DV_B)
    return qa, ka, va, logf, qb, kb, vb, gate_a, gate_b

def fox_attend(q, cq, qpos, k, v, ck, kpos):
    s = jnp.einsum('bqhd,bshd->bhqs', q, k).astype(jnp.float32) * (DH_A ** -0.5)
    decay = jnp.swapaxes(cq, 1, 2)[..., :, None] - jnp.swapaxes(ck, 1, 2)[..., None, :]
    mask = kpos[None, :] <= qpos[:, None]
    s = jnp.where(mask, s + decay, -jnp.inf)
    p = jax.nn.softmax(s, axis=-1)
    return jnp.einsum('bhqs,bshd->bqhd', p.astype(v.dtype), v)

def diff_lambda(lq1, lk1, lq2, lk2):
    f32 = jnp.float32
    return (jnp.exp(jnp.sum(lq1.astype(f32) * lk1.astype(f32)))
            - jnp.exp(jnp.sum(lq2.astype(f32) * lk2.astype(f32))) + LAMBDA_INIT)

def diff_attend(q, qpos, k, v, kpos, lam):
    s = jnp.einsum('bqhmd,bshmd->bhmqs', q, k).astype(jnp.float32) * (DH_B ** -0.5)
    dist = jnp.abs(qpos[:, None] - kpos[None, :]).astype(jnp.float32)
    slopes = jnp.asarray(ALIBI_SLOPES)[:, None, None, None]
    mask = (kpos // CHUNK)[None, :] <= (qpos // CHUNK)[:, None]
    s = jnp.where(mask, s - slopes * dist, -jnp.inf)
    p = jax.nn.softmax(s, axis=-1)
    a = p[:, :, 0] - lam * p[:, :, 1]
    return jnp.einsum('bhqs,bshe->bqhe', a.astype(v.dtype), v)

def branch_merge(x, oa, ob, gate_a, gate_b, subln_b, w_oa, w_ob, w_out):
    B, T, _ = x.shape
    ob = rms_norm(ob, subln_b) * (1.0 - LAMBDA_INIT)
    ya = oa.reshape(B, T, W_A) @ w_oa
    yb = ob.reshape(B, T, W_B) @ w_ob
    m = jax.nn.sigmoid(gate_a) * ya + jax.nn.sigmoid(gate_b) * yb
    return x + m @ w_out

def conv_ffn(x, prev_u, g_ffn, w_up, conv_w, conv_b, w_down):
    T = x.shape[1]
    u = rms_norm(x, g_ffn) @ w_up
    up = jnp.concatenate([prev_u, u], axis=1)
    c = conv_w[0] * up[:, :T] + conv_w[1] * up[:, 1:T + 1] + conv_w[2] * up[:, 2:T + 2] + conv_b
    a, b = jnp.split(c, 2, axis=-1)
    out = (jax.nn.silu(a) * b) @ w_down
    return x + out, up[:, -(CONV_W - 1):]

def setup_inputs(seed: int = 0) -> dict:
    key = jax.random.key(seed)
    keys = jax.random.split(key, 28)
    def n(i, shape, scale):
        return scale * jax.random.normal(keys[i], shape, jnp.float32)
    return {
        'x_prompt': n(0, (BATCH, SEQ, D_MODEL), 1.0),
        'x_sample': n(1, (DEC_BATCH, DEC_SEQ, D_MODEL), 1.0),
        'cache_a_k': n(2, (DEC_BATCH, PAST_LEN, H_A, DH_A), 1.0),
        'cache_a_v': n(3, (DEC_BATCH, PAST_LEN, H_A, DH_A), 1.0),
        'cache_a_logf': jax.nn.log_sigmoid(2.0 + n(4, (DEC_BATCH, PAST_LEN, H_A), 1.0)),
        'cache_b_k': n(5, (DEC_BATCH, PAST_LEN, H_B, 2, DH_B), 1.0),
        'cache_b_v': n(6, (DEC_BATCH, PAST_LEN, H_B, DV_B), 1.0),
        'state_ffn_conv': n(7, (DEC_BATCH, CONV_W - 1, 2 * D_FF), 1.0),
        'g_attn': 1.0 + n(8, (D_MODEL,), 0.1),
        'w_in': n(9, (D_MODEL, N_IN), D_MODEL ** -0.5),
        'b_f': 2.0 + n(10, (H_A,), 0.5),
        'qn_a': 1.0 + n(11, (DH_A,), 0.1),
        'kn_a': 1.0 + n(12, (DH_A,), 0.1),
        'qn_b': 1.0 + n(13, (DH_B,), 0.1),
        'kn_b': 1.0 + n(14, (DH_B,), 0.1),
        'lambda_q1': n(15, (DH_B,), 0.1),
        'lambda_k1': n(16, (DH_B,), 0.1),
        'lambda_q2': n(17, (DH_B,), 0.1),
        'lambda_k2': n(18, (DH_B,), 0.1),
        'subln_b': 1.0 + n(19, (DV_B,), 0.1),
        'w_oa': n(20, (W_A, D_MODEL), W_A ** -0.5),
        'w_ob': n(21, (W_B, D_MODEL), W_B ** -0.5),
        'w_out': n(22, (D_MODEL, D_MODEL), D_MODEL ** -0.5),
        'g_ffn': 1.0 + n(23, (D_MODEL,), 0.1),
        'w_up': n(24, (D_MODEL, 2 * D_FF), D_MODEL ** -0.5),
        'conv_w': n(25, (CONV_W, 2 * D_FF), CONV_W ** -0.5),
        'conv_b': n(26, (2 * D_FF,), 0.01),
        'w_down': n(27, (D_FF, D_MODEL), D_FF ** -0.5),
    }

def reference(x_prompt, x_sample, cache_a_k, cache_a_v, cache_a_logf, cache_b_k, cache_b_v,
              state_ffn_conv, g_attn, w_in, b_f, qn_a, kn_a, qn_b, kn_b,
              lambda_q1, lambda_k1, lambda_q2, lambda_k2, subln_b, w_oa, w_ob, w_out,
              g_ffn, w_up, conv_w, conv_b, w_down):
    lam = diff_lambda(lambda_q1, lambda_k1, lambda_q2, lambda_k2)

    B, T, _ = x_prompt.shape
    qa, ka, va, logf, qb, kb, vb, ga, gb = mixer_inputs(x_prompt, g_attn, w_in, b_f, qn_a, kn_a, qn_b, kn_b)
    c = jnp.cumsum(logf, axis=1)
    pos = jnp.arange(T)
    nb = T // Q_BLOCK
    blk = lambda a: jnp.swapaxes(a.reshape((B, nb, Q_BLOCK) + a.shape[2:]), 0, 1)
    unblk = lambda a: jnp.swapaxes(a, 0, 1).reshape((B, T) + a.shape[3:])
    pos_blk = pos.reshape(nb, Q_BLOCK)
    oa = unblk(lax.map(lambda t: fox_attend(t[0], t[1], t[2], ka, va, c, pos), (blk(qa), blk(c), pos_blk)))
    ob = unblk(lax.map(lambda t: diff_attend(t[0], t[1], kb, vb, pos, lam), (blk(qb), pos_blk)))
    x1 = branch_merge(x_prompt, oa, ob, ga, gb, subln_b, w_oa, w_ob, w_out)
    y_prompt, p_conv = conv_ffn(x1, jnp.zeros((B, CONV_W - 1, 2 * D_FF), x1.dtype), g_ffn, w_up, conv_w, conv_b, w_down)

    Ts = x_sample.shape[1]
    P = cache_a_k.shape[1]
    qa_s, ka_s, va_s, logf_s, qb_s, kb_s, vb_s, ga_s, gb_s = mixer_inputs(x_sample, g_attn, w_in, b_f, qn_a, kn_a, qn_b, kn_b)
    qpos = P + jnp.arange(Ts)
    kpos = jnp.arange(P + Ts)
    ka_all = jnp.concatenate([cache_a_k.astype(ka_s.dtype), ka_s], axis=1)
    va_all = jnp.concatenate([cache_a_v.astype(va_s.dtype), va_s], axis=1)
    c_all = jnp.cumsum(jnp.concatenate([cache_a_logf.astype(jnp.float32), logf_s], axis=1), axis=1)
    kb_all = jnp.concatenate([cache_b_k.astype(kb_s.dtype), kb_s], axis=1)
    vb_all = jnp.concatenate([cache_b_v.astype(vb_s.dtype), vb_s], axis=1)
    oa_s = fox_attend(qa_s, c_all[:, P:], qpos, ka_all, va_all, c_all, kpos)
    ob_s = diff_attend(qb_s, qpos, kb_all, vb_all, kpos, lam)
    x1s = branch_merge(x_sample, oa_s, ob_s, ga_s, gb_s, subln_b, w_oa, w_ob, w_out)
    y_sample, s_conv = conv_ffn(x1s, state_ffn_conv.astype(x1s.dtype), g_ffn, w_up, conv_w, conv_b, w_down)

    return (y_prompt, y_sample,
            ka, va, logf.astype(x_prompt.dtype), kb, vb, p_conv,
            ka_s, va_s, logf_s.astype(x_sample.dtype), kb_s, vb_s, s_conv)


_drawn_inputs = setup_inputs


def setup_inputs(seed=0):
    import zlib

    import numpy as np

    out = dict(_drawn_inputs(seed))
    spreads = {}
    factors = {'cache_a_logf': 4.407, 'qn_a': 3.28, 'lambda_k2': 4.028, 'conv_b': 8.0}
    for name, (base, spread) in spreads.items():
        noise = np.random.default_rng([zlib.crc32(name.encode()), seed]).standard_normal(out[name].shape)
        drawn = base * np.exp(spread * noise) if base else spread * noise
        out[name] = __import__('jax').numpy.asarray(drawn.astype(out[name].dtype))
    for name, factor in factors.items():
        out[name] = (out[name] * factor).astype(out[name].dtype)
    return out
```

```python
import math
from contextlib import ExitStack

import numpy as np
import concourse.bass as bass
from concourse import mybir

F32 = mybir.dt.float32
F32R = mybir.dt.float32r
I32 = mybir.dt.int32
ALU = mybir.AluOpType
ACT = mybir.ActivationFunctionType
AX = mybir.AxisListType.X

P = 128
D = 1024
T_P = 1024
T_S = 64
T = T_P + T_S
PAST = 1024
KB = D // P
DH = 64
H_A = 8
W_A = 512
W_B = 512
D_FF = 2816
FB = D_FF // P
EPS = 1e-6
LAMBDA_INIT = 0.8 - 0.6 * math.exp(-0.3 * (1 - 1))
BIG = 2.0 ** 100
NT = 9
CHUNKS = [(0, 364), (364, 364), (728, 360)]
Z_QA, Z_KA, Z_VA, Z_F = 0, W_A, 2 * W_A, 3 * W_A
Z_QB = 3 * W_A + H_A
Z_KB, Z_VB = Z_QB + W_B, Z_QB + 2 * W_B
Z_G = Z_QB + 3 * W_B
UNITS = 8
TILES = [7, 8, 6, 5, 4, 3, 2, 1, 0]
GROUPS = [6, 6, 5, 5]
PASSES = [(0, 0), (0, 1), (1, 0)]

PROLOGUE_PLAN = [("W", "F"), ("W", "Q"), "F0", "F1", "F2", ("FORGET",), ("W", "K"), "Q0", "Q1", "Q2", ("W", "V"),
                 "K0", "K1", "K2", "SS0", "SS1", ("NORM",), "V0", "V1", "V2", "NQ0", "NQ1", "NQ2", "NK0", "NK1", "NK2",
                 ("SCALE",), "VT0", "VT1", "VT2", "KT0", "KT1", "KT2", ("SPLIT",), "KC0", "KC1", ("WFIRST",)]
PROLOGUE_JOBS = [x for x in PROLOGUE_PLAN if isinstance(x, str)]
PROLOGUE_BLOCKS = {"F": (1, 1), "Q": (2, 0), "K": (3, 1), "V": (4, 0)}


def unit_plan(kind, nxt):
    if kind == "A":
        gaps = {-1: [["Q0"], ["Q1"]], 7: [["Q2"], ["SS0", "K0"]], 8: [["K1"], ["K2"]], 6: [["SS1", "V0"], ["V1"]],
                5: [["V2"], ["NQ0", "NQ1"]], 4: [["VT0", "VT1"], ["VT2", "NQ2"]], 3: [["G00"], ["NK0", "NK1"]],
                2: [["G01"], ["NK2"]], 1: [["G02"], ["KT0", "KT1"]], 0: [["G10"], ["KT2"]]}
    elif nxt:
        gaps = {-1: [["Q0"], ["Q1"]], 7: [["Q2"], ["K0"]], 8: [["SS0"], ["K1"]], 6: [["K2"], ["SS1", "V0"]],
                5: [["V1"], ["V2"]], 4: [["VT0", "VT1"], ["VT2", "G00"]], 3: [["NQ0", "NQ1"], ["G01"]],
                2: [["NQ2", "NK0"], ["G02"]], 1: [["NK1", "NK2"], ["G10"]], 0: [["KT0", "KT1"], ["KT2"]]}
    else:
        gaps = {-1: [["G00"], []], 7: [[], ["G01"]], 8: [["/G02"], ["G02"]], 6: [[], ["G10"]], 5: [[], ["G11"]],
                4: [[], ["G12"]], 3: [[], []], 2: [[], []], 1: [[], []], 0: [[], []]}
    end = ["SPLIT", "G11", "G12", "KC0", "KC1", "OT0", "OT1", "OT2"] if nxt else ["OT0", "OT1", "OT2"]
    then = {"SS1": [("ROOT",)], "NK2": [], **({"G02": [("H", "FIRST")]} if nxt else {}),
            **{a: [("H", b)] for a, b in WEIGHTS_AFTER[nxt].items()}}
    later = {"SS1": [("RD",)], "NK2": [("SCALE",)], **({"G02": [("L", "FIRST")]} if nxt else {}),
             **{a: [("L", b)] for a, b in WEIGHTS_AFTER[nxt].items()}}
    pending = []
    plan = [("GS",)]

    def jobs(names):
        for n in names:
            if n == "SPLIT":
                plan.append((n,))
            elif n[0] == "/":
                plan.append(("HALF", n[1:]))
            else:
                plan.append(("J", n))
                plan.extend(then.get(n, []))
                pending.extend(later.get(n, []))

    def flush():
        plan.extend(pending)
        pending.clear()

    plan.append(("S", 7, 0))
    jobs(gaps[-1][0])
    plan.append(("S", 7, 1))
    jobs(gaps[-1][1])
    plan.append(("VC",))
    flush()
    if kind == "B":
        plan.append(("C", 7))
    for n, i in enumerate(TILES):
        after = TILES[n + 1] if n + 1 < NT else None
        g = gaps[i]
        plan.append(("T", i, 0))
        if after is not None:
            plan.append(("S", after, 0))
        jobs(g[0])
        plan.append(("AV", i, 0))
        flush()
        if kind == "A":
            plan.append(("T", i, 1))
        if after is not None:
            plan.append(("S", after, 1))
        jobs(g[1])
        if kind == "A":
            plan.append(("AV", i, 1))
            flush()
        elif after is not None:
            plan.append(("C", after))
    plan.append(("OFIN",))
    flush()
    jobs(end)
    assert not pending
    return plan


WEIGHTS_AFTER = {True: {"Q0": "K", "K0": "V", "V2": "G0", "G00": "G1"}, False: {"G00": "G1"}}
BLOCKS = {True: ["Q", "K", "V", "G0", "G1"], False: ["G0", "G1"]}
SLOT = {"FIRST": 0, "Q": 0, "K": 1, "V": 0, "G0": 0, "G1": 1}


def plan_index(plan):
    job, s, grp = {}, {}, {}
    for it in plan:
        if it[0] == "J":
            job[it[1]] = len(job) + 1
        elif it[0] == "S":
            s[it[1:]] = len(s) + 1
        elif it[0] == "T":
            grp[it[1:]] = len(grp) + 1
    return job, s, grp


def keys_of(i):
    return PAST + T_S if i == 8 else P * (i + 1)


def build(nc, ins, outs):
    ctx = ExitStack()
    sem = lambda n: ctx.enter_context(nc.semaphore(n))

    (x_p, x_s, c_ak, c_av, c_alogf, c_bk, c_bv, st_conv, g_attn, w_in, b_f, qn_a, kn_a, qn_b, kn_b,
     l_q1, l_k1, l_q2, l_k2, subln, w_oa, w_ob, w_out, g_ffn, w_up, conv_w, conv_b, w_down) = ins
    (y_p, y_s, p_ak, p_av, p_alogf, p_bk, p_bv, p_conv, s_ak, s_av, s_alogf, s_bk, s_bv, s_conv) = outs
    w_in_v = w_in.rearrange("(k p) n -> p k n", p=P)
    col = lambda a, t: a.rearrange("o (t p) (u h) d -> u (o p) t (h d)", t=t, h=2)

    def heads(a, tiles):
        if len(a.shape) == 5:
            return a.rearrange("o (t p) u m d -> u (o p) t (m d)", t=tiles)
        if a.shape[3] == P:
            return a.rearrange("o (t p) u d -> u (o p) t d", t=tiles)
        return a.rearrange("o (t p) (u h) d -> u (o p) t (h d)", t=tiles, h=2)

    x_scr = nc.dram_tensor("x_scr", (KB, P, T), F32).ap()
    gate_scr = nc.dram_tensor("gate_scr", (16, P, T), F32).ap()
    o_scr = nc.dram_tensor("o_scr", (UNITS, P, T), F32).ap()
    c_scr = nc.dram_tensor("c_scr", (2, H_A, T), F32).ap()

    def alloc(stack):
        return (lambda n, s, d=F32: stack.enter_context(nc.sbuf_tensor(n, s, d)),
                lambda n, s: stack.enter_context(nc.psum_tensor(n, s, F32)))

    sb, pb = alloc(ctx)
    ident = sb("ident", [P, P])
    vecs = sb("vecs", [P, 6 * 44 + 16])
    taps = [vecs[:, 44 * i:44 * i + 44] for i in range(3)]
    cbias = vecs[:, 132:176]
    cstate = vecs[:, 176:264]
    gain_attn, gain_ffn = vecs[:, 264:272], vecs[:, 272:280]
    small = sb("small", [P, 48])
    eps_t = small[:, 0:1]
    gq_a, gk_a, gq_b, gk_b = (small[:, i:i + 1] for i in range(1, 5))
    sub_g = small[:, 5:6]
    neg_lam = small[:, 6:7]
    den = small[:, 8:10]
    rden = small[:, 10:12]
    smin = small[:, 12:14]
    sumsq = small[:, 16:25]
    rsub = small[:, 26:35]
    meansq = sb("meansq", [P, NT, 2, 2])
    root = sb("root", [P, NT, 2, 2])
    inv0 = sb("inv0", [P, NT])
    bf_t = small[0:H_A, 36:37]
    one_t = small[:, 40:41]
    gains_raw = small[:, 37:39]
    xact = ExitStack()

    banks = [pb(f"bank{i}", [P, 512]) for i in range(2)]
    psS = pb("psS", [P, 3 * 512])
    psT = pb("psT", [P, 2 * 512])
    psO = pb("psO", [P, 512])
    TGROUPS = [range(0, 3), range(3, 6), range(6, 9)]
    ring_u = [banks[0], banks[1], psS[:, 0:512], psS[:, 512:1024], psS[:, 1024:1536], psO]
    ring_d = [banks[0], banks[1], psO]
    three = [psS[:, 512 * c:512 * c + CHUNKS[c][1]] for c in range(3)]

    sb_n, _ = alloc(xact)
    xn = [sb_n("xn_hi", [P, KB, T], F32R), sb_n("xn_lo", [P, KB, T], F32R)]
    wraw = sb_n("wraw", [P, KB, P])
    wsp = [[sb_n(f"w_{'hl'[h]}{s}", [P, KB, P], F32R) for h in range(2)] for s in range(2)]
    ident_r = sb_n("ident_r", [P, P], F32R)
    mask_r = sb_n("mask_r", [P, P], F32R)
    dist = sb_n("dist", [P, T])
    half_ones = sb_n("half_ones", [P, P])

    s1 = ExitStack()
    sb1, _ = alloc(s1)
    x_tm = sb1("x_tm", [P, NT, D])
    xT = sb1("xT", [P, KB, T])
    sq1 = [sb1(f"sq1_{i}", [P, T]) for i in range(2)]
    rstd1 = sb1("rstd1", [P, T])
    rows = sb1("rows", [44, 8, P])
    all_ones = sb1("all_ones", [P, P])
    dist_i = sb1("dist_i", [P, T], I32)
    lamv = sb1("lamv", [P, 4, DH])
    lamt = sb1("lamt", [P, 2 * DH + 4])
    maskf = sb1("maskf", [P, P])
    clog_tm = sb1("clog_tm", [P, 8, H_A])
    clog = sb1("clog", [H_A, PAST])
    s1.close()
    s1b = ExitStack()
    sb1b, _ = alloc(s1b)
    fz = sb1b("fz", [H_A, T])
    fa = sb1b("fa", [H_A, T])
    fones = sb1b("fones", [H_A, T])
    logf = sb1b("logf", [H_A, T])
    csum = sb1b("csum", [H_A, 2, T])
    lf_tm = sb1b("lf_tm", [P, NT, H_A])
    s1b.close()

    s2 = ExitStack()
    sb2, _ = alloc(s2)
    qs = [sb2(f"q_{'hl'[h]}", [P, T], F32R) for h in range(2)]
    ks = [sb2(f"k_{'hl'[h]}", [P, T], F32R) for h in range(2)]
    v_hl = sb2("v_hl", [P, NT, 2, P], F32R)
    kcs = [sb2(f"kc_{'hl'[h]}", [P, PAST], F32R) for h in range(2)]
    vc_hl = sb2("vc_hl", [P, 8, 2, P], F32R)
    zq, zk, zv = (sb2(n, [P, T]) for n in ("zq", "zk", "zv"))
    sqq, sqk = (sb2(n, [P, T]) for n in ("sqq", "sqk"))
    v_tm = sb2("v_tm", [P, NT, P])
    k_tm = sb2("k_tm", [P, NT, P])
    o_tm = sb2("o_tm", [P, NT, P])
    junk = sb2("junk", [P, P])
    sc = [sb2(f"sc{m}", [P, T]) for m in range(2)]
    pt = [sb2(f"pT_{'hl'[h]}", [P, NT, P], F32R) for h in range(2)]
    cum_p = [sb2(f"cum_p{m}", [P, T_P]) for m in range(2)]
    cum_s = [sb2(f"cum_s{m}", [P, T]) for m in range(2)]
    vc_raw = sqk[:, 0:PAST].rearrange("p (t c) -> p t c", c=P)
    gate_st = [zv, sqq]
    oT_st = sqk
    s2.close()
    xact.close()

    s3 = ExitStack()
    sb3, _ = alloc(s3)
    wraw3 = [sb3(f"wraw3_{s}", [P, KB, P]) for s in range(2)]
    wsp3 = [[sb3(f"w3_{'hl'[h]}{s}", [P, KB, P], F32R) for h in range(2)] for s in range(2)]
    s3r = ExitStack()
    sb3r, _ = alloc(s3r)
    o_all = sb3r("o_all", [P, UNITS, T])
    s3r.close()
    s3m = ExitStack()
    sb3m, _ = alloc(s3m)
    ms = [sb3m(f"m_{'hl'[h]}", [P, KB, T], F32R) for h in range(2)]
    s3o = ExitStack()
    sb3o, _ = alloc(s3o)
    os_ = [sb3o(f"o_{'hl'[h]}", [P, KB, T], F32R) for h in range(2)]
    gates = [sb3o(f"gate{i}", [P, T]) for i in range(2)]
    mt = [[sb3o(f"m_{'ab'[g]}{x}", [P, 364]) for g in range(2)] for x in range(2)]
    s3o.close()
    s4 = ExitStack()
    sb4, _ = alloc(s4)
    x1 = sb4("x1", [P, KB, T])
    ones4 = sb4("ones4", [P, P])
    x_in = [sb4(f"x_in{i}", [P, T]) for i in range(2)]
    sq4 = [sb4(f"sq4_{i}", [P, T]) for i in range(2)]
    rstd4 = sb4("rstd4", [P, T])
    s4.close()
    s3m.close()
    s5 = ExitStack()
    sb5, _ = alloc(s5)
    x2s = [sb5(f"x2_{'hl'[h]}", [P, KB, T], F32R) for h in range(2)]
    sb5("x1_stays", [P, KB, T])
    gsp = [sb5(f"g_{'hl'[h]}", [P, max(GROUPS), T], F32R) for h in range(2)]
    TU = T + 4
    ub = [sb5(f"u{i}", [P, NT * P + 8]) for i in range(2)]
    edges = sb5("edges", [P, 4, 2 * FB])
    edge_rows = sb5("edge_rows", [4 * FB, 2, P])
    ct = [sb5(f"ct{i}", [P, TU - 2]) for i in range(2)]
    y_blk = [c[:, 0:T] for c in ct]
    y_tm = [u[:, 0:NT * P].rearrange("p (t c) -> p t c", c=P) for u in ub]
    s5.close()
    s3.close()

    names = ("ld_vec ld_x ld_xs ld_small ld_clog lf_out c_out x_out "
             "idt cst dst msk vecT vecD xT_f xT_e sq_d ms_f sqrt1 rstd_d xh_s xl_s xh_d pool1 "
             "fz_e fchain lf_d csum_d clT_f clT_e lfT_f lfT_e lam_v lam_a small_d vpad "
             "wraw_s wh_d wl_d pj_f pj_d kcl_d s_f s_d p_d rd_d cb_d t_f th_d tl_d av_f o_d om_d "
             "rs_d of_d sq_rt rt_d norm_d sph_d spl_d vch_d vcl_d dch st_v st_k st_g0 st_g1 st_o ld_vc ld_kc ld_cum "
             "w3_s0 w3_s1 w3h w3l ld_o0 ld_o1 oh_d ol_d mg_f mg_d ld_g gmul m_h m_l ld_xi0 ld_xi1 wo_f x1_d sq4_d "
             "ms4_f sqrt4 r4_d t4_s x2h x2l on4 up_f up_free u_free edge_d edge_o edgeT_f edgeT_e ct_a c1_d silu_d gm_d gh_d gl_free dn_f dn_free "
             "dst_a dst_m idr ms_pad hold_pe yT_f yT_free y_o0 y_o1 pads hold_dve hold_pool dchain").split()
    S = {n: sem(n) for n in names}

    def wait(e, name, value):
        if isinstance(value, int) and value <= 0:
            return
        e.wait_ge(S[name], value)

    def hold(e, name, value, own):
        if isinstance(value, int) and value <= 0:
            return
        e.wait_ge(S[name], value)
        e.sem_inc(S[own], 1)

    PLANS = {(k, n): unit_plan(k, n) for k, n in (("A", True), ("B", True), ("B", False))}
    INDEX = {kn: plan_index(p) for kn, p in PLANS.items()}
    JOBS1 = PROLOGUE_JOBS
    J_PRO, J_UNIT = len(JOBS1), len(INDEX["A", True][0])
    assert J_PRO % 2 == 0 and J_UNIT % 2 == 0 and J_UNIT == len(INDEX["B", True][0])
    J1 = {n: i + 1 for i, n in enumerate(JOBS1)}

    class Unit:
        def __init__(self, u, kind, nxt):
            self.u, self.kind, self.nxt = u, kind, nxt
            self.plan = PLANS[kind, nxt]
            self.job, self.s, self.grp = INDEX[kind, nxt]
            self.next_kind = None if not nxt else ("B" if kind == "B" or (isinstance(u, int) and u == 3) else "A")
            self.j0 = u * J_UNIT + J_PRO
            self.w0 = u * 5 + 4
            self.s0 = u * 18
            self.g0 = u * 18 if kind == "A" else u * 9 + 36

        def block(self, name):
            return self.w0 + (6 if name == "FIRST" else BLOCKS[self.nxt].index(name) + 1)

    def units(e, body):
        with e.Fori(0, 3) as u:
            body(Unit(u, "A", True))
        body(Unit(3, "A", True))
        with e.Fori(4, 7) as u:
            body(Unit(u, "B", True))
        body(Unit(7, "B", False))

    block = ctx.enter_context(nc.Block())

    @block.sync
    def _(sp):
        sp.dma_start(x_tm[:, 0:8, :], x_p.rearrange("o (t p) d -> (o p) t d", p=P)).then_inc(S["ld_x"], 16)
        sp.dma_start(x_tm[0:T_S, 8, :], x_s[0]).then_inc(S["ld_xs"], 16)

        def load_w(dst, b, src):
            wait(sp, "wl_d", b - 1)
            sp.dma_start(dst, src).then_inc(S["wraw_s"], 16)

        for n, c in enumerate([Z_F, Z_QA, Z_KA, Z_VA]):
            load_w(wraw[:], n + 1, w_in_v[:, :, c:c + P])

        def cols(base, first, u):
            if isinstance(u, int):
                at = base + (u - first) * P
                return w_in_v[:, :, at:at + P]
            lo = base - first * P
            view = w_in_v[:, :, lo % P:lo % P + (5128 - lo % P) // P * P].rearrange("p k (u c) -> u p k c", c=P)
            return view[u + lo // P]

        def body(U):
            if U.nxt:
                to_b = U.next_kind == "B"
                for base in ([Z_QB, Z_KB, Z_VB] if to_b else [Z_QA, Z_KA, Z_VA]):
                    load_w(wraw[:], U.block("QKV"[[Z_QB, Z_KB, Z_VB, Z_QA, Z_KA, Z_VA].index(base) % 3]),
                           cols(base, 4 if to_b else 0, U.u + 1))
            gv = w_in_v[:, :, Z_G:].rearrange("p k (u g c) -> u g p k c", g=2, c=P)
            for g in range(2):
                load_w(wraw[:], U.block(f"G{g}"), gv[U.u][g])

        units(sp, body)

        wait(sp, "pj_f", J_PRO + 7 * J_UNIT + INDEX["B", False][0]["G12"])
        oa = w_oa.rearrange("(k p) (i s c) -> i s p k c", p=P, c=P, s=2)
        ob = w_ob.rearrange("(k p) (i s c) -> i s p k c", p=P, c=P, s=2)
        wo = w_out.rearrange("(k p) (i s c) -> i s p k c", p=P, c=P, s=2)
        for s in range(2):
            sp.dma_start(wraw3[s][:, 0:4, :], oa[0][s]).then_inc(S[f"w3_s{s}"], 16)
            sp.dma_start(wraw3[s][:, 4:8, :], ob[0][s]).then_inc(S[f"w3_s{s}"], 16)
        with sp.Fori(1, 4) as i:
            for s in range(2):
                sp.wait_ge(S["w3l"], i * 2 + (s - 1))
                sp.dma_start(wraw3[s][:, 0:4, :], oa[i][s]).then_inc(S[f"w3_s{s}"], 16)
                sp.dma_start(wraw3[s][:, 4:8, :], ob[i][s]).then_inc(S[f"w3_s{s}"], 16)
        with sp.Fori(4, 8) as i:
            for s in range(2):
                sp.wait_ge(S["w3l"], i * 2 + (s - 1))
                sp.dma_start(wraw3[s][:], wo[i - 4][s]).then_inc(S[f"w3_s{s}"], 16)
        base, f0 = 8, 0
        up = w_up.rearrange("(k p) (h j c) -> j h p k c", p=P, c=P, h=2)
        dn = w_down.rearrange("(k p) (i s c) -> i s p k c", p=P, c=P, s=2)
        for ng in GROUPS:
            with sp.Fori(0, ng) as i:
                for s in range(2):
                    sp.wait_ge(S["w3l"], i * 2 + (2 * base + s - 1))
                    sp.dma_start(wraw3[s][:], up[i + f0][s]).then_inc(S[f"w3_s{s}"], 16)
            base += ng
            with sp.Fori(0, 4) as i:
                for s in range(2):
                    sp.wait_ge(S["w3l"], i * 2 + (2 * base + s - 1))
                    sp.dma_start(wraw3[s][:, 0:ng, :], dn[i][s][:, f0:f0 + ng, :]).then_inc(S[f"w3_s{s}"], 16)
            base += 4
            f0 += ng

    @block.gpsimd
    def _(pool):
        pool.memset(ident[:], 0.0).then_inc(S["idt"], 1)
        pool.wait_ge(S["idt"], 1)
        pool.affine_select(out=ident[:], in_=ident[:], compare_op=ALU.not_equal, fill=1.0, base=0,
                           pattern=[[-1, P]], channel_multiplier=1).then_inc(S["idt"], 1)
        pool.memset(all_ones[:], 1.0 / D).then_inc(S["cst"], 1)
        pool.memset(eps_t, EPS).then_inc(S["cst"], 1)
        for i in range(6):
            src = [conv_w[0], conv_w[1], conv_w[2], conv_b, st_conv[0, 0], st_conv[0, 1]][i]
            pool.dma_start(rows[:, i, :], src.rearrange("(b c) -> b c", c=P)).then_inc(S["ld_vec"], 16)
        for i, g in ((6, g_attn), (7, g_ffn)):
            pool.dma_start(rows[0:KB, i, :], g.rearrange("(b c) -> b c", c=P)).then_inc(S["ld_vec"], 16)
        for i, g in enumerate((qn_a, kn_a, qn_b, kn_b)):
            for h in range(2):
                pool.dma_start(small[DH * h:DH * h + DH, 1 + i:2 + i],
                               g.rearrange("(p a) -> p a", a=1)).then_inc(S["ld_small"], 16)
        pool.dma_start(sub_g, subln.rearrange("(p a) -> p a", a=1)).then_inc(S["ld_small"], 16)
        pool.dma_start(bf_t, b_f.rearrange("(p a) -> p a", a=1)).then_inc(S["ld_small"], 16)
        for i, l in enumerate((l_q1, l_k1, l_q2, l_k2)):
            pool.dma_start(lamv[:, i, :], l.rearrange("(a d) -> a d", a=1).broadcast_to([P, DH])).then_inc(S["ld_small"], 16)
        pool.dma_start(clog_tm[:], c_alogf.rearrange("o (t p) h -> (o p) t h", p=P)).then_inc(S["ld_clog"], 16)
        pool.iota(dist_i[:], pattern=[[-1, T]], base=T - P, channel_multiplier=1).then_inc(S["dst"], 1)
        pool.memset(half_ones[:], 0.0).then_inc(S["cst"], 1)
        pool.wait_ge(S["cst"], 3)
        pool.memset(half_ones[0:DH, 0:DH], 1.0 / DH).then_inc(S["cst"], 1)
        pool.memset(half_ones[DH:P, DH:P], 1.0 / DH).then_inc(S["cst"], 1)
        pool.wait_ge(S["cst"], 5)
        pool.memset(maskf[:], 0.0).then_inc(S["msk"], 1)
        pool.wait_ge(S["msk"], 1)
        pool.affine_select(out=maskf[:], in_=maskf[:], compare_op=ALU.is_ge, fill=BIG, base=0,
                           pattern=[[-1, P]], channel_multiplier=1).then_inc(S["msk"], 1)
        for k in range(KB):
            pool.wait_ge(S["xT_e"], 3 * k + 3)
            pool.dma_start(x_scr[k], xT[:, k, :]).then_inc(S["x_out"], 16)
        pool.wait_ge(S["fchain"], 1)
        pool.memset(fones[:], 1.0).then_inc(S["pool1"], 1)
        pool.wait_ge(S["csum_d"], 3)
        pool.dma_start(c_scr[0, :, 0:T_P], csum[:, 0, 0:T_P]).then_inc(S["c_out"], 16)
        pool.dma_start(c_scr[1], csum[:, 1, :]).then_inc(S["c_out"], 16)
        pool.wait_ge(S["lfT_e"], 1)
        pool.dma_start(p_alogf.rearrange("o (t p) h -> (o p) t h", p=P), lf_tm[:, 0:8, :]).then_inc(S["lf_out"], 16)
        pool.dma_start(s_alogf[0], lf_tm[0:T_S, 8, :]).then_inc(S["lf_out"], 16)
        pool.wait_ge(S["x_out"], 16 * KB)
        pool.wait_ge(S["xl_s"], KB)
        pool.memset(v_tm[DH:P, 8, :], 0.0).then_inc(S["vpad"], 1)

        def store_kv(which, to, un, tile, count):
            hold(pool, "pj_d", count, "hold_pool")
            a, b = {("A", "v"): (p_av, s_av), ("A", "k"): (p_ak, s_ak),
                    ("B", "v"): (p_bv, s_bv), ("B", "k"): (p_bk, s_bk)}[to, which]
            pool.dma_start(heads(a, 8)[un], tile[:, 0:8, :]).then_inc(S["st_" + which], 16)
            pool.dma_start(heads(b, 1)[un], tile[0:T_S, 8:9, :]).then_inc(S["st_" + which], 16)

        def load_kc(to, un, value):
            hold(pool, "st_k", value, "hold_pool")
            pool.dma_start(k_tm[:, 0:8, :], heads(c_ak if to == "A" else c_bk, 8)[un]).then_inc(S["ld_kc"], 16)

        def load_cum(un):
            for m in range(2):
                cu = lambda a: c_scr[a].rearrange("(u m) t -> u m t", m=2)[un][m:m + 1, :]
                pool.dma_start(cum_p[m][:], cu(0)[:, 0:T_P].broadcast_to([P, T_P])).then_inc(S["ld_cum"], 16)
                pool.dma_start(cum_s[m][:], cu(1).broadcast_to([P, T])).then_inc(S["ld_cum"], 16)

        store_kv("v", "A", 0, v_tm, J1["VT2"])
        store_kv("k", "A", 0, k_tm, J1["KT2"])
        load_kc("A", 0, 32)
        pool.wait_ge(S["c_out"], 32)
        load_cum(0)

        def body(U):
            u, loc = U.u, (U.u if U.kind == "A" else U.u - 4)
            hold(pool, "st_o", u * 16, "hold_pool")
            hold(pool, "norm_d", u + 1, "hold_pool")
            pool.dma_start(vc_raw, heads(c_av if U.kind == "A" else c_bv, 8)[loc]).then_inc(S["ld_vc"], 16)
            if U.nxt:
                nk = U.next_kind
                un = (0 if nk != U.kind else loc + 1)
                store_kv("v", nk, un, v_tm, U.j0 + U.job["VT2"])
                store_kv("k", nk, un, k_tm, U.j0 + U.job["KT2"])
                load_kc(nk, un, u * 32 + 64)
                if nk == "A":
                    hold(pool, "s_d", U.s0 + 18, "hold_pool")
                    load_cum(un)
            for g in range(2):
                hold(pool, "pj_d", U.j0 + U.job[f"G{g}2"], "hold_pool")
                pool.dma_start(gate_scr.rearrange("(u g) p t -> u g p t", g=2)[u][g], gate_st[g][:]
                               ).then_inc(S[f"st_g{g}"], 16)
                if g == 0 and U.nxt:
                    hold(pool, "pj_d", U.j0 + U.job["OT2"], "hold_pool")
                    pool.dma_start(o_scr[u], oT_st[:]).then_inc(S["st_o"], 16)

        units(pool, body)
        pool.wait_ge(S["pj_f"], J_PRO + 7 * J_UNIT + INDEX["B", False][0]["G12"])
        pool.wait_ge(S["st_o"], 16 * 7)
        pool.dma_start(o_all[:, 0:7, :], o_scr[0:7].rearrange("u p t -> p u t")).then_inc(S["ld_o0"], 16)
        pool.wait_ge(S["pj_d"], J_PRO + 7 * J_UNIT + INDEX["B", False][0]["OT2"])
        pool.dma_start(o_scr[7], oT_st[:]).then_inc(S["st_o"], 16)
        pool.wait_ge(S["st_o"], 16 * 8)
        pool.dma_start(o_all[:, 7, :], o_scr[7]).then_inc(S["ld_o1"], 16)
        pool.wait_ge(S["av_f"], 72 + 36)
        pool.wait_ge(S["st_g0"], 16 * 8)
        pool.wait_ge(S["st_g1"], 16 * 8)
        pool.wait_ge(S["om_d"], 72 + 36)
        for fb in range(KB):
            wait(pool, "gmul", 3 * fb)
            for g in range(2):
                pool.dma_start(gates[g][:], gate_scr[g * KB + fb]).then_inc(S["ld_g"], 16)
        pool.wait_ge(S["mg_f"], 3 * KB)
        pool.wait_ge(S["gmul"], 3 * KB)
        pool.wait_ge(S["m_l"], 3 * KB)
        pool.memset(ones4[:], 1.0 / D).then_inc(S["on4"], 1)
        for fb in range(KB):
            if fb >= 2:
                pool.wait_ge(S["x1_d"], 3 * (fb - 1))
            pool.dma_start(x_in[fb % 2][:], x_scr[fb]).then_inc(S[f"ld_xi{fb % 2}"], 16)
        pool.wait_ge(S["edgeT_e"], 2)
        for x, out in enumerate((p_conv, s_conv)):
            pool.dma_start(out[0].rearrange("r (b c) -> (r b) c", c=P), edge_rows[:, x, :]).then_inc(S["edge_o"], 16)
        yp = y_p.rearrange("o (t p) (i s c) -> i s (o p) t c", p=P, c=P, s=2)
        ys = y_s.rearrange("o p (i s c) -> i s (o p) c", c=P, s=2)
        with pool.Fori(0, 4) as i:
            for s in range(2):
                hold(pool, "yT_free", i * 6 + (3 * s + 6), "hold_pool")
                pool.dma_start(yp[i][s], y_tm[s][:, 0:8, :]).then_inc(S[f"y_o{s}"], 16)
                pool.dma_start(ys[i][s], y_tm[s][0:T_S, 8, :]).then_inc(S[f"y_o{s}"], 16)
        for name, value in (("lf_out", 32), ("st_v", 32 * 8), ("st_k", 32 * 8), ("edge_o", 32),
                            ("y_o0", 128), ("y_o1", 128)):
            pool.wait_ge(S[name], value)

    @block.tensor
    def _(pe):
        def mm(out, w, x, first, last, **kw):
            return pe.matmul(out, w, x, start=first, stop=last, **kw)

        def split_product(out, ws, xs, kblocks, tok, lo=0, hi=None):
            steps = [(k, ab) for k in kblocks for ab in PASSES]
            for i in range(lo, len(steps) if hi is None else hi):
                k, (a, b) = steps[i]
                r = mm(out, ws[a][:, k, :], xs[b][:, k, tok], i == 0, i == len(steps) - 1)
            return r

        pe.wait_ge(S["idt"], 2)
        pe.wait_ge(S["ld_vec"], 16 * 8)
        for i in range(6):
            pe.transpose(psO[:, 44 * i:44 * i + 44], rows[0:44, i, :], ident[0:44, 0:44])
        for i in (6, 7):
            r = pe.transpose(psO[:, 264 + 8 * (i - 6):272 + 8 * (i - 6)], rows[0:KB, i, :], ident[0:KB, 0:KB])
        r.then_inc(S["vecT"], 1)
        pe.wait_ge(S["ld_clog"], 16)
        for t in range(8):
            r = pe.transpose(psT[0:H_A, P * t:P * t + P], clog_tm[:, t, :], ident[:])
        r.then_inc(S["clT_f"], 1)
        pe.wait_ge(S["ld_x"], 16)
        pe.wait_ge(S["ld_xs"], 16)

        def square_sums(k):
            pe.wait_ge(S["sq_d"], k + 1)
            if k == 0:
                pe.wait_ge(S["cst"], 1)
            for c, (c0, n) in enumerate(CHUNKS):
                r = mm(three[c], all_ones[:], sq1[k % 2][:, c0:c0 + n], k == 0, k == KB - 1)
            r.then_inc(S["ms_f"], 1)

        for k in range(KB):
            if k == 0:
                pe.wait_ge(S["clT_e"], 1)
                pe.wait_ge(S["vecD"], 1)
            for part, (t0, t1, out) in enumerate(((0, 4, psT[:, 0:512]), (4, 8, psT[:, 512:1024]), (8, 9, psO[:, 0:T_S]))):
                wait(pe, "xT_e", 3 * (k - 1) + part + 1)
                for t in range(t0, t1):
                    if t < 8:
                        r = pe.transpose(out[:, P * (t - t0):P * (t - t0) + P], x_tm[:, t, P * k:P * k + P], ident[:])
                    else:
                        r = pe.transpose(out, x_tm[0:T_S, 8, P * k:P * k + P], ident[0:T_S, 0:T_S])
                r.then_inc(S["xT_f"], 1)
            if k >= 1:
                square_sums(k - 1)
        square_sums(KB - 1)

        def proj(bank, block_no, slot, c, lo, hi):
            if c == 0 and lo == 0:
                pe.wait_ge(S["wl_d"], block_no)
            c0, m = CHUNKS[c]
            return split_product(bank[:, 0:m], wsp[slot], xn, range(KB), slice(c0, c0 + m), lo, hi)

        def transposed(bank, src, tiles, tail_rows=T_S):
            for j, t in enumerate(tiles):
                n = T_S if t == 8 else P
                r = pe.transpose(bank[0:n, P * j:P * j + P], src[:, P * t:P * t + n], ident[:])
            return r


        def job(name, n, idx, base_of, U=None, lo=0, hi=None):
            bank = banks[(idx - 1) % 2]
            if lo == 0:
                wait(pe, "pj_d", n - 2)
                if U is not None and U.nxt:
                    for x in range(2):
                        if idx - 2 == U.job[f"KC{x}"]:
                            pe.wait_ge(S["kcl_d"], U.u * 2 + (3 + x))
            kind, c = name[:-1], int(name[-1])
            if kind in ("F", "Q", "K", "V", "G0", "G1"):
                if U is None:
                    no, slot = PROLOGUE_BLOCKS[kind]
                else:
                    no, slot = U.block(kind), SLOT[kind]
                    if idx <= 2 and lo == 0:
                        pe.wait_ge(S["kcl_d"], U.u * 2 + 2)
                r = proj(bank, no, slot, c, lo, hi)
                if hi is not None:
                    return
            elif kind == "SS":
                pe.wait_ge(S["pj_d"], base_of("QK"[c] + "2"))
                if U is None and c == 0:
                    pe.wait_ge(S["cst"], 5)
                for t in range(NT):
                    m = T_S if t == 8 else P
                    r = mm(bank[0:m, 2 * t:2 * t + 2], (sqq, sqk)[c][:, P * t:P * t + m], half_ones[:, 0:P:DH], True, True)
            elif kind in ("NQ", "NK"):
                if name == "NQ0":
                    pe.wait_ge(S["rt_d"], 1 if U is None else U.u + 2)
                pe.sem_inc(S["hold_pe"], 1)
                for j, t in enumerate(TGROUPS[c]):
                    m = T_S if t == 8 else P
                    for h in range(2):
                        src = root[0:m, t, "QK".index(kind[1]), h:h + 1].broadcast_to([m, DH])
                        r = mm(bank[DH * h:DH * h + DH, P * j:P * j + m], src, ident[0:m, 0:m], True, True)
            elif kind == "VT":
                pe.wait_ge(S["pj_d"], base_of("V2"))
                r = transposed(bank, zv, TGROUPS[c])
            elif kind == "KT":
                pe.wait_ge(S["norm_d"], 1 if U is None else U.u + 2)
                r = transposed(bank, zk, TGROUPS[c])
            elif kind == "KC":
                pe.wait_ge(S["ld_kc"], 16 if U is None else U.u * 16 + 32)
                for j in range(4):
                    r = pe.transpose(bank[:, P * j:P * j + P], k_tm[:, 4 * c + j, :], ident[:])
            elif kind == "OT":
                if U.kind == "A":
                    pe.wait_ge(S["om_d"], U.g0 + 18)
                else:
                    pe.wait_ge(S["of_d"], U.u - 3)
                for j, t in enumerate(TGROUPS[c]):
                    r = pe.transpose(bank[:, P * j:P * j + P], o_tm[:, t, :], ident[:])
            r.then_inc(S["pj_f"], 1)

        for it in PROLOGUE_PLAN:
            if isinstance(it, str):
                if it == "F0":
                    pe.wait_ge(S["xl_s"], KB)
                job(it, J1[it], J1[it], lambda name: J1[name])
                if it == "F2":
                    pass
                if it == "V2":
                    pe.wait_ge(S["lf_d"], 1)
                    for t in range(NT):
                        n = T_S if t == 8 else P
                        r = pe.transpose(psO[0:n, 8 * t:8 * t + 8], logf[:, P * t:P * t + n], ident[0:H_A, 0:H_A])
                    r.then_inc(S["lfT_f"], 1)

        def body(U):
            u = U.u
            begun = None
            for it in U.plan:
                if it[0] in ("HALF", "J"):
                    idx = U.job[it[1]]
                    lo, hi = (12 if it[1] == begun else 0), (12 if it[0] == "HALF" else None)
                    job(it[1], U.j0 + idx, idx, lambda name: U.j0 + U.job[name], U, lo, hi)
                    begun = it[1] if it[0] == "HALF" else None
                elif it[0] == "S":
                    i, m = it[1:]
                    s = U.s[i, m]
                    wait(pe, "s_d", U.s0 + (s - 1))
                    if s == 1:
                        pe.wait_ge(S["spl_d"], u * 3 + 3)
                        if not isinstance(u, int) or u == 0:
                            pe.wait_ge(S["idr"], 2)
                    hr = slice(DH * m, DH * m + DH)
                    if i == 8:
                        q0, parts = T - P, [(kcs, 0, 512, 0), (kcs, 512, 512, 512), (ks, T_P, T_S, T_P)]
                        if m == 0:
                            pe.wait_ge(S["kcl_d"], u * 2 + 2)
                        diag, mcols = (T_P, T), slice(DH, P)
                    else:
                        q0, n = P * i, P * (i + 1)
                        parts = [(ks, c, min(512, n - c), c) for c in range(0, n, 512)]
                        diag, mcols = (P * i, P * i + P), slice(0, P)
                    for src, k0, n, at in parts:
                        masked = U.kind == "A" and at <= diag[0] < at + n
                        for x, (a, b) in enumerate(PASSES):
                            r = mm(psS[:, at:at + n], qs[a][hr, q0:q0 + P], src[b][hr, k0:k0 + n],
                                   x == 0, x == 2 and not masked)
                        if masked:
                            r = mm(psS[:, diag[0]:diag[1]], ident_r[:], mask_r[:, mcols], False, True)
                    r.then_inc(S["s_f"], 1)
                elif it[0] == "T":
                    i, m = it[1:]
                    g = U.g0 + U.grp[i, m]
                    if U.kind == "A":
                        pe.wait_ge(S["p_d"], U.s0 + U.s[i, m])
                    else:
                        pe.wait_ge(S["cb_d"], U.grp[i, m] + (U.u * 9 - 36))
                    wait(pe, "tl_d", g - 1)
                    src = sc[m]
                    if i == 8:
                        wait(pe, "o_d", g - 1)
                    for kb in range(8 if i == 8 else i + 1):
                        r = pe.transpose(psT[:, P * kb:P * kb + P], src[:, P * kb:P * kb + P], ident[:])
                    if i == 8:
                        r = pe.transpose(psO[0:T_S, 256:384], src[:, T_P:T], ident[:])
                    r.then_inc(S["t_f"], 1)
                elif it[0] == "AV":
                    i, m = it[1:]
                    g = U.g0 + U.grp[i, m]
                    pe.wait_ge(S["tl_d"], g)
                    wait(pe, "o_d", g - 1)
                    vc = slice(DH * m, DH * m + DH) if U.kind == "A" else slice(0, P)
                    w = vc.stop - vc.start
                    if i == 8:
                        if m == 0:
                            pe.wait_ge(S["vcl_d"], u + 1)
                        parts = [(vc_hl, kb, kb, P) for kb in range(8)] + [(v_hl, 8, 8, T_S)]
                    else:
                        parts = [(v_hl, kb, kb, P) for kb in range(i + 1)]
                    for x, (src, kb, tb, nk) in enumerate(parts):
                        last = x == len(parts) - 1
                        mm(psO[:, 0:2 * w], pt[0][0:nk, tb, :], src[0:nk, kb, :, vc], x == 0, False)
                        r = mm(psO[:, 0:w], pt[1][0:nk, tb, :], src[0:nk, kb, 0, vc], False, last)
                    r.then_inc(S["av_f"], 1)

        units(pe, body)

        pe.wait_ge(S["ol_d"], UNITS)
        pe.wait_ge(S["o_d"], 108)

        def merge(i):
            for s in range(2):
                n3 = i * 2 + s
                pe.wait_ge(S["w3l"], n3 + 1)
                for c, (c0, m) in enumerate(CHUNKS):
                    j = i * 6 + (3 * s + c)
                    if not isinstance(i, int) or j >= 2:
                        pe.wait_ge(S["gmul"], j - 1)
                    x = (3 * s + c) % 2
                    tok = slice(c0, c0 + m)
                    split_product(psS[:, 512 * x:512 * x + m], wsp3[s], os_, range(0, 4), tok)
                    split_product(psT[:, 512 * x:512 * x + m], wsp3[s], os_, range(4, 8), tok).then_inc(S["mg_f"], 1)

        merge(0)
        with pe.Fori(1, 4) as i:
            merge(i)

        pe.wait_ge(S["m_l"], 3 * KB)
        pe.wait_ge(S["on4"], 1)

        def sums4(fb):
            pe.wait_ge(S["sq4_d"], fb + 1)
            for c, (c0, n) in enumerate(CHUNKS):
                r = mm(three[c], ones4[:], sq4[fb % 2][:, c0:c0 + n], fb == 0, fb == KB - 1)
            r.then_inc(S["ms4_f"], 1)

        for fb in range(KB):
            pe.wait_ge(S["w3l"], KB + fb + 1)
            for c, (c0, m) in enumerate(CHUNKS):
                j = 3 * fb + c
                wait(pe, "x1_d", j - 1)
                split_product(banks[j % 2][:, 0:m], wsp3[fb % 2], ms, range(KB), slice(c0, c0 + m)).then_inc(S["wo_f"], 1)
            if fb >= 1:
                sums4(fb - 1)
        sums4(KB - 1)

        pe.wait_ge(S["x2l"], KB)
        pe.wait_ge(S["sqrt4"], 3)
        blk, f0 = 2 * KB, 0
        for gi, ng in enumerate(GROUPS):
            pe.wait_ge(S["dn_free"], 24 * gi + 3)
            with pe.Fori(0, ng) as i:
                for h in range(2):
                    pe.wait_ge(S["w3l"], i * 2 + (blk + h + 1))
                    for c, (c0, m) in enumerate(CHUNKS):
                        x = 3 * h + c
                        n = i * 6 + (6 * f0 + x)
                        pe.wait_ge(S["up_free"], n + 1)
                        split_product(ring_u[x][:, 0:m], wsp3[h], x2s, range(KB), slice(c0, c0 + m)
                                      ).then_inc(S["up_f"], 1)
            f0 += ng
            blk += 2 * ng
            pe.wait_ge(S["gl_free"], f0 + 1)
            pe.wait_ge(S["up_free"], 6 * f0 + 6)
            if f0 == FB:
                pe.wait_ge(S["edge_d"], 2 * FB)
                for x in range(2):
                    pe.transpose(psT[0:4 * FB, 512 * x:512 * x + P], edges[:, 2 * x:2 * x + 2, :].rearrange("p r b -> p (r b)"),
                                 ident[:]).then_inc(S["edgeT_f"], 1)
            with pe.Fori(0, 4) as i:
                for s in range(2):
                    pe.wait_ge(S["w3l"], i * 2 + (blk + s + 1))
                    for c, (c0, m) in enumerate(CHUNKS):
                        x = 3 * s + c
                        pe.wait_ge(S["dn_free"], i * 6 + (24 * gi + x + 1))
                        split_product(ring_d[x % 3][:, 0:m], wsp3[s], gsp, range(ng), slice(c0, c0 + m)
                                      ).then_inc(S["dn_f"], 1)
                    if gi == len(GROUPS) - 1:
                        if s == 0:
                            pe.wait_ge(S["edgeT_e"], 2)
                        for part, out in enumerate((psT[:, 0:512], psT[:, 512:1024], psS[:, 0:512])):
                            x = 3 * s + part
                            pe.wait_ge(S["yT_free"], i * 6 + (x + 1))
                            if part == 0:
                                pe.wait_ge(S["dn_free"], i * 6 + (24 * gi + 3 * s + 6))
                            for j, t in enumerate(TGROUPS[part]):
                                n = T_S if t == 8 else P
                                r = pe.transpose(out[0:n, P * j:P * j + P], y_blk[s][:, P * t:P * t + n], ident[:])
                            r.then_inc(S["yT_f"], 1)
            blk += 8

    @block.scalar
    def _(act):
        def copy(out, in_, **kw):
            return act.activation(out, in_, ACT.Copy, **kw)

        act.wait_ge(S["idt"], 2)
        copy(ident_r[:], ident[:]).then_inc(S["idr"], 1)
        act.wait_ge(S["msk"], 2)
        copy(mask_r[:], maskf[:]).then_inc(S["idr"], 1)
        act.wait_ge(S["dst"], 1)
        act.activation(dist[:], dist_i[:], ACT.Abs).then_inc(S["dst_a"], 1)
        act.wait_ge(S["vecT"], 1)
        copy(vecs[:, 0:280], psO[:, 0:280]).then_inc(S["vecD"], 1)
        act.wait_ge(S["clT_f"], 1)
        copy(clog[:], psT[0:H_A, 0:PAST]).then_inc(S["clT_e"], 1)
        act.wait_ge(S["lam_v"], 3)
        act.activation(lamt[:, 130:132], lamt[:, 128:130], ACT.Exp).then_inc(S["lam_a"], 1)

        def split_w(value, used_sem, used):
            act.wait_ge(S["wraw_s"], value * 16)
            if used_sem:
                act.wait_ge(S[used_sem], used)
            return value

        for k in range(KB):
            for part, (a, b, src) in enumerate(((0, 512, psT[:, 0:512]), (512, 1024, psT[:, 512:1024]), (1024, T, psO[:, 0:T_S]))):
                act.wait_ge(S["xT_f"], 3 * k + part + 1)
                copy(xT[:, k, a:b], src).then_inc(S["xT_e"], 1)
        act.wait_ge(S["ms_f"], KB)
        act.wait_ge(S["cst"], 2)
        for c, (c0, n) in enumerate(CHUNKS):
            act.activation(rstd1[:, c0:c0 + n], three[c], ACT.Sqrt, bias=eps_t).then_inc(S["sqrt1"], 1)

        def w_high(slot, number, sem_name=None, value=None):
            act.wait_ge(S["wraw_s"], number * 16)
            if sem_name:
                act.wait_ge(S[sem_name], value)
            copy(wsp[slot][0][:], wraw[:]).then_inc(S["wh_d"], 1)

        w_high(1, 1)
        for k in range(KB):
            act.wait_ge(S["xh_d"], k + 1)
            copy(xn[0][:, k, :], sq1[k % 2][:]).then_inc(S["xh_s"], 1)
            if k == 3:
                w_high(0, 2)

        def evacuate(name, n, idx, base_of, U=None):
            bank = banks[(idx - 1) % 2]
            kind, c = name[:-1], int(name[-1])
            u = 0 if U is None else U.u + 1
            act.wait_ge(S["pj_f"], n)
            if kind in ("F", "Q", "K", "V", "G0", "G1"):
                c0, m = CHUNKS[c]
                src, tok = bank[:, 0:m], slice(c0, c0 + m)
            if kind == "F":
                if c == 0:
                    act.wait_ge(S["small_d"], 1)
                r = act.activation(fz[:, tok], bank[0:H_A, 0:m], ACT.Identity, bias=bf_t)
            elif kind in ("Q", "K"):
                z, q = (zq, sqq) if kind == "Q" else (zk, sqk)
                if c == 0:
                    if U is None:
                        act.wait_ge(S["x_out"], 16 * KB)
                        act.wait_ge(S["xl_s"], KB)
                    else:
                        act.wait_ge(S["spl_d"], U.u * 3 + 3)
                        if kind == "Q":
                            wait(act, "st_g1", U.u * 16)
                        else:
                            act.wait_ge(S["vcl_d"], U.u + 1)
                copy(z[:, tok], src)
                r = act.activation(q[:, tok], src, ACT.Square)
            elif kind == "V":
                if c == 0 and U is not None:
                    wait(act, "st_g0", U.u * 16)
                r = copy(zv[:, tok], src)
            elif kind == "SS":
                r = copy(meansq[:, 0:8, c, :], bank[:, 0:16].rearrange("p (t h) -> p t h", h=2))
                r = copy(meansq[0:T_S, 8, c, :], bank[0:T_S, 16:18])
            elif kind in ("NQ", "NK"):
                t0, m = TGROUPS[c][0] * P, (3 * P if c < 2 else 2 * P + T_S)
                r = copy((sqq if kind == "NQ" else sqk)[:, t0:t0 + m], bank[:, 0:m])
            elif kind in ("VT", "KT"):
                dst = v_tm if kind == "VT" else k_tm
                if c == 0 and U is not None:
                    if kind == "VT":
                        act.wait_ge(S["st_v"], U.u * 32 + 32)
                        act.wait_ge(S["spl_d"], U.u * 3 + 3)
                    else:
                        act.wait_ge(S["st_k"], U.u * 32 + 32)
                whole = 3 if c < 2 else 2
                r = copy(dst[:, 3 * c:3 * c + whole, :], bank[:, 0:whole * P].rearrange("p (t c) -> p t c", c=P))
                if c == 2:
                    r = copy(dst[0:T_S, 8, :], bank[0:T_S, 2 * P:3 * P])
            elif kind == "KC":
                if U is not None:
                    act.wait_ge(S["s_f"], U.s0 + 18)
                r = copy(kcs[0][:, 512 * c:512 * c + 512], bank[:])
            elif kind in ("G0", "G1"):
                g = int(kind[1])
                if c == 0 and not U.nxt:
                    act.wait_ge(S[f"st_g{g}"], U.u * 16)
                if c == 0 and U.nxt and g == 1:
                    act.wait_ge(S["norm_d"], U.u + 2)
                r = act.activation(gate_st[g][:, tok], src, ACT.Tanh, scale=0.5)
            elif kind == "OT":
                if c == 0:
                    act.wait_ge(S["vcl_d"], U.u + 1)
                kw = {} if U.kind == "A" else {"scale": sub_g}
                whole = (3 if c < 2 else 2) * P
                r = copy(oT_st[:, 3 * P * c:3 * P * c + whole], bank[:, 0:whole], **kw)
                if c == 2:
                    r = copy(oT_st[:, T_P:T], bank[:, 2 * P + DH:3 * P], **kw)
            r.then_inc(S["pj_d"], 1)

        def norm_roots(U=None):
            act.wait_ge(S["pj_d"], J1["SS1"] if U is None else U.j0 + U.job["SS1"])
            if U is None:
                act.wait_ge(S["ms_pad"], 1)
            else:
                act.wait_ge(S["pj_f"], U.j0)
            act.activation(root[:], meansq[:], ACT.Sqrt, bias=eps_t).then_inc(S["sq_rt"], 1)

        def split_qkv(U=None):
            if U is None:
                act.wait_ge(S["norm_d"], 1)
                act.wait_ge(S["lf_out"], 32)
                act.wait_ge(S["c_out"], 32)
                act.wait_ge(S["pj_d"], J1["VT2"])
                act.wait_ge(S["vpad"], 1)
            else:
                act.wait_ge(S["norm_d"], U.u + 2)
                act.wait_ge(S["s_f"], U.s0 + 18)
                act.wait_ge(S["av_f"], U.g0 + (18 if U.kind == "A" else 9))
                act.wait_ge(S["pj_d"], U.j0 + U.job["VT2"])
            copy(qs[0][:], zq[:]).then_inc(S["sph_d"], 1)
            copy(ks[0][:], zk[:]).then_inc(S["sph_d"], 1)
            copy(v_hl[:, :, 0, :], v_tm[:]).then_inc(S["sph_d"], 1)

        for it in PROLOGUE_PLAN:
            if isinstance(it, str):
                evacuate(it, J1[it], J1[it], lambda name: J1[name])
                if it == "V2":
                    act.wait_ge(S["lfT_f"], 1)
                    copy(lf_tm[:, 0:8, :], psO[:, 0:64].rearrange("p (t h) -> p t h", h=8))
                    copy(lf_tm[0:T_S, 8, :], psO[0:T_S, 64:72]).then_inc(S["lfT_e"], 1)
            elif it[0] == "FORGET":
                act.wait_ge(S["pj_d"], J1["F2"])
                act.activation(fa[:], fz[:], ACT.Abs).then_inc(S["fz_e"], 1)
                act.wait_ge(S["fz_e"], 1)
                act.activation(fa[:], fa[:], ACT.Exp, scale=-1.0).then_inc(S["fz_e"], 1)
                act.wait_ge(S["fz_e"], 2)
                act.activation(fa[:], fa[:], ACT.Ln, bias=one_t[0:H_A]).then_inc(S["fz_e"], 1)
            elif it[0] == "W" and it[1] in ("K", "V"):
                no, slot = PROLOGUE_BLOCKS[it[1]]
                w_high(slot, no, "pj_f", J1["F2" if it[1] == "K" else "Q2"])
            elif it[0] == "WFIRST":
                w_high(0, 5, "pj_f", J1["V2"])
            elif it[0] == "NORM":
                norm_roots()
            elif it[0] == "SPLIT":
                split_qkv()

        def body(U):
            u = U.u
            for it in U.plan:
                if it[0] == "J":
                    idx = U.job[it[1]]
                    evacuate(it[1], U.j0 + idx, idx, lambda name: U.j0 + U.job[name], U)
                elif it[0] == "VC":
                    act.wait_ge(S["ld_vc"], u * 16 + 16)
                    wait(act, "av_f", U.g0)
                    copy(vc_hl[:, :, 0, :], vc_raw).then_inc(S["vch_d"], 1)
                elif it[0] == "S":
                    i, m = it[1:]
                    n = keys_of(i)
                    act.wait_ge(S["s_d"], U.s0 + U.s[i, m])
                    act.activation(sc[m][:, 0:n], sc[m][:, 0:n], ACT.Exp, bias=smin[:, m:m + 1], scale=-1.0,
                                   accum_out=den[:, m:m + 1]).then_inc(S["p_d"], 1)
                elif it[0] == "T":
                    i, m = it[1:]
                    g = U.g0 + U.grp[i, m]
                    act.wait_ge(S["t_f"], g)
                    wait(act, "av_f", g - 1)
                    nb = 8 if i == 8 else i + 1
                    r = copy(pt[0][:, 0:nb, :], psT[:, 0:P * nb].rearrange("p (t c) -> p t c", c=P))
                    if i == 8:
                        r = copy(pt[0][0:T_S, 8, :], psO[0:T_S, 256:384])
                    r.then_inc(S["th_d"], 1)
                elif it[0] == "AV":
                    i, m = it[1:]
                    g = U.g0 + U.grp[i, m]
                    act.wait_ge(S["o_d"], g)
                    if U.kind == "A":
                        act.wait_ge(S["rd_d"], g)
                        part = o_tm[:, i, DH * m:DH * m + DH]
                        copy(part, part, scale=rden[:, m:m + 1]).then_inc(S["om_d"], 1)
                    else:
                        act.activation(junk[:], o_tm[:, i, :], ACT.Square, scale=inv0[:, i:i + 1],
                                       accum_out=sumsq[:, i:i + 1]).then_inc(S["om_d"], 1)
                elif it[0] == "H":
                    name = it[1]
                    before = {"K": U.j0, "V": U.j0 + U.job.get("Q2", 0), "G0": U.j0 + U.job.get("V2", 0),
                              "G1": U.j0 + U.job.get("K2", 0), "FIRST": U.j0 + U.job["G02"]}[name]
                    w_high(SLOT[name], U.block(name), "pj_f", before)
                elif it[0] == "ROOT":
                    norm_roots(U)
                elif it[0] == "SPLIT":
                    split_qkv(U)
                elif it[0] == "OFIN" and U.kind == "B":
                    act.wait_ge(S["om_d"], U.g0 + 9)
                    act.activation(rsub, sumsq, ACT.Sqrt, bias=eps_t, scale=1.0 / P).then_inc(S["rs_d"], 1)

        units(act, body)

        def w3_high(s, loaded, sem_name, value):
            act.wait_ge(S[f"w3_s{s}"], loaded)
            wait(act, sem_name, value)
            copy(wsp3[s][0][:], wraw3[s][:]).then_inc(S["w3h"], 1)

        last = J_PRO + 7 * J_UNIT
        w3_high(0, 32, "pj_f", last + INDEX["B", False][0]["G12"])
        w3_high(1, 32, "pj_f", last)
        act.wait_ge(S["st_o"], 128)
        act.wait_ge(S["st_v"], 256)
        act.wait_ge(S["st_k"], 256)
        act.wait_ge(S["av_f"], 108)
        act.wait_ge(S["o_d"], 108)
        act.wait_ge(S["of_d"], 4)
        for k in range(UNITS):
            act.wait_ge(S["ld_o0" if k < 7 else "ld_o1"], 16)
            copy(os_[0][:, k, :], o_all[:, k, :]).then_inc(S["oh_d"], 1)

        def merge(i):
            for s in range(2):
                for c, (c0, m) in enumerate(CHUNKS):
                    j, x = i * 6 + (3 * s + c), (3 * s + c) % 2
                    act.wait_ge(S["mg_d"], j + 1)
                    if isinstance(i, int) and j == 0:
                        act.wait_ge(S["ol_d"], UNITS)
                    copy(ms[0][:, i * 2 + s, c0:c0 + m], mt[x][0][:, 0:m], scale=0.5).then_inc(S["m_h"], 1)
                w3_high(s, (i * 32 + 64) if (isinstance(i, int) and i < 3) or not isinstance(i, int) else 144,
                        "mg_f", i * 6 + (3 * s + 3))

        merge(0)
        with act.Fori(1, 3) as i:
            merge(i)
        merge(3)

        for fb in range(KB):
            act.wait_ge(S["x1_d"], 3 * fb + 3)
            wait(act, "ms4_f", fb - 1)
            act.activation(sq4[fb % 2][:], x1[:, fb, :], ACT.Square).then_inc(S["sq4_d"], 1)
            w3_high(fb % 2, 128 + 16 * (fb // 2 + 2), "wo_f", 3 * fb + 3)
        act.wait_ge(S["ms4_f"], KB)
        for c, (c0, n) in enumerate(CHUNKS):
            act.activation(rstd4[:, c0:c0 + n], three[c], ACT.Sqrt, bias=eps_t).then_inc(S["sqrt4"], 1)
        for k in range(KB):
            act.wait_ge(S["t4_s"], k + 1)
            copy(x2s[0][:, k, :], sq4[k % 2][:]).then_inc(S["x2h"], 1)

        act.sem_inc(S["up_free"], 6)
        act.sem_inc(S["yT_free"], 3)
        act.wait_ge(S["x2l"], KB)
        act.wait_ge(S["pads"], 4)
        pair, f0 = 8, 0
        state = cstate.rearrange("p (r b) -> p b r", r=2)
        for gi, ng in enumerate(GROUPS):
            if gi:
                act.wait_ge(S["dn_f"], 24 * gi)
            with act.Fori(0, ng) as i:
                done = i * 6 + 6 * f0
                for h in range(2):
                    act.wait_ge(S["u_free"], i * 2 + (2 * f0 + h + 1))
                    copy(ub[h][:, T_P + 2:T_P + 4], state[:, i + (f0 + FB * h), :])
                    for c, (c0, m) in enumerate(CHUNKS):
                        x = 3 * h + c
                        act.wait_ge(S["up_f"], i * 6 + (6 * f0 + x + 1))
                        src = ring_u[x]
                        if c < 2:
                            r = copy(ub[h][:, c0 + 2:c0 + 2 + m], src[:, 0:m])
                        else:
                            copy(ub[h][:, c0 + 2:T_P + 2], src[:, 0:T_P - c0])
                            r = copy(ub[h][:, T_P + 4:TU], src[:, T_P - c0:m])
                        r.then_inc(S["up_free"], 1)
                    act.wait_ge(S[f"w3_s{h}"], i * 16 + (64 + 16 * (pair + 2)))
                    copy(wsp3[h][0][:], wraw3[h][:]).then_inc(S["w3h"], 1)
                    if h == 1:
                        act.wait_ge(S["u_free"], i * 2 + (2 * f0 + 3))
                        act.activation(ct[0][:], ct[0][:], ACT.Silu).then_inc(S["silu_d"], 1)
                    act.wait_ge(S["up_free"], i * 6 + (6 * f0 + 3 * h + 9))
                    act.wait_ge(S["gl_free"], i + (f0 + 1))
                    b = i + (f0 + FB * h)
                    act.activation(ct[h][:], ub[h][:, 2:TU], ACT.Identity, scale=taps[2][:, bass.ds(b, 1)],
                                   bias=cbias[:, bass.ds(b, 1)]).then_inc(S["ct_a"], 1)
                act.wait_ge(S["gm_d"], i + (f0 + 1))
                copy(gsp[0][:, i, 0:T_P], ct[1][:, 0:T_P])
                copy(gsp[0][:, i, T_P:T], ct[1][:, T_P + 2:TU - 2]).then_inc(S["gh_d"], 1)
            pair += ng
            f0 += ng
            final = gi == len(GROUPS) - 1
            if final:
                for x in range(2):
                    act.wait_ge(S["edgeT_f"], x + 1)
                    copy(edge_rows[:, x, :], psT[0:4 * FB, 512 * x:512 * x + P]).then_inc(S["edgeT_e"], 1)

            def down(i):
                for s in range(2):
                    if not (final and isinstance(i, int) and i == 3):
                        act.wait_ge(S[f"w3_s{s}"], i * 16 + (64 + 16 * (pair + 2)))
                        act.wait_ge(S["dn_f"], i * 6 + (24 * gi + 3 * s + 3))
                        copy(wsp3[s][0][:], wraw3[s][:]).then_inc(S["w3h"], 1)
                    if final:
                        wait(act, f"y_o{s}", i * 32)
                        for part in range(3):
                            act.wait_ge(S["yT_f"], i * 6 + (3 * s + part + 1))
                            bank = (psT[:, 0:512], psT[:, 512:1024], psS[:, 0:512])[part]
                            whole = 3 if part < 2 else 2
                            r = copy(y_tm[s][:, 3 * part:3 * part + whole, :],
                                     bank[:, 0:whole * P].rearrange("p (t c) -> p t c", c=P))
                            if part == 2:
                                r = copy(y_tm[s][0:T_S, 8, :], bank[0:T_S, 2 * P:3 * P])
                            r.then_inc(S["yT_free"], 1)

            if final:
                down(0)
                with act.Fori(1, 3) as i:
                    down(i)
                down(3)
            else:
                with act.Fori(0, 4) as i:
                    down(i)
            pair += 4

    @block.vector
    def _(dve):
        chain = [0]

        def link(ins, name="fchain"):
            chain[0] += 1
            ins.then_inc(S["dchain"], 1)
            dve.wait_ge(S["dchain"], chain[0])

        def high_of(t):
            return t.bitcast(F32)

        def rest(out, in_, high):
            return dve.tensor_tensor(out, in_, high_of(high), ALU.subtract)

        dve.memset(one_t, 1.0)
        dve.memset(meansq[:, 8, :, :], 1.0).then_inc(S["ms_pad"], 1)
        dve.wait_ge(S["ld_small"], 16 * 14)
        dve.tensor_scalar(gq_a, gq_a, -DH ** -0.5, None, ALU.mult)
        dve.tensor_scalar(gq_b, gq_b, -DH ** -0.5, None, ALU.mult)
        dve.tensor_scalar(sub_g, sub_g, 1.0 - LAMBDA_INIT, None, ALU.mult).then_inc(S["small_d"], 1)
        dve.tensor_tensor(lamt[:, 0:DH], lamv[:, 0, :], lamv[:, 1, :], ALU.mult).then_inc(S["lam_v"], 1)
        dve.tensor_tensor(lamt[:, DH:2 * DH], lamv[:, 2, :], lamv[:, 3, :], ALU.mult).then_inc(S["lam_v"], 1)
        dve.wait_ge(S["lam_v"], 2)
        dve.tensor_reduce(out=lamt[:, 128:130], in_=lamt[:, 0:128].rearrange("p (a d) -> p a d", a=2),
                          axis=AX, op=ALU.add).then_inc(S["lam_v"], 1)
        dve.wait_ge(S["lam_a"], 1)
        link(dve.tensor_tensor(neg_lam, lamt[:, 131:132], lamt[:, 130:131], ALU.subtract))
        link(dve.tensor_scalar(neg_lam, neg_lam, -LAMBDA_INIT, None, ALU.add))
        dve.wait_ge(S["dst_a"], 1)
        dve.memset(dist[0:DH, T - DH:T], BIG).then_inc(S["dst_m"], 1)

        for k in range(KB):
            dve.wait_ge(S["xT_e"], 3 * k + 3)
            wait(dve, "ms_f", k - 1)
            dve.tensor_tensor(sq1[k % 2][:], xT[:, k, :], xT[:, k, :], ALU.mult).then_inc(S["sq_d"], 1)
        dve.wait_ge(S["sqrt1"], 3)
        link(dve.reciprocal(rstd1[:], rstd1[:]))

        def w_low(slot, number):
            dve.wait_ge(S["wh_d"], number)
            rest(wsp[slot][1][:], wraw[:], wsp[slot][0][:]).then_inc(S["wl_d"], 1)

        def x_scaled(k):
            wait(dve, "xh_s", k - 1)
            dve.scalar_tensor_tensor(sq1[k % 2][:], xT[:, k, :], gain_attn[:, k:k + 1], rstd1[:],
                                     ALU.mult, ALU.mult).then_inc(S["xh_d"], 1)

        def x_low(k):
            dve.wait_ge(S["xh_s"], k + 1)
            rest(xn[1][:, k, :], sq1[k % 2][:], xn[0][:, k, :]).then_inc(S["xl_s"], 1)

        dve.wait_ge(S["ms_f"], KB)
        dve.wait_ge(S["vecD"], 1)
        x_scaled(0)
        w_low(1, 1)
        for k in range(1, KB):
            if k >= 2:
                dve.wait_ge(S["xl_s"], k - 1)
            x_scaled(k)
            x_low(k - 1)
        x_low(KB - 1)
        w_low(0, 2)

        def invert_roots(U=None):
            dve.wait_ge(S["sq_rt"], 1 if U is None else U.u + 2)
            dve.reciprocal(root[:], root[:]).then_inc(S["rt_d"], 1)

        def normalize(U=None):
            kind = "A" if U is None else U.next_kind
            for name, z, q, g in (("NQ2", zq, sqq, gq_a if kind == "A" else gq_b),
                                  ("NK2", zk, sqk, gk_a if kind == "A" else gk_b)):
                dve.wait_ge(S["pj_d"], J1[name] if U is None else U.j0 + U.job[name])
                r = dve.scalar_tensor_tensor(z[:], z[:], g, q[:], ALU.mult, ALU.mult)
            r.then_inc(S["norm_d"], 1)

        def split_qkv(U=None):
            n = 0 if U is None else U.u * 3 + 3
            dve.wait_ge(S["sph_d"], n + 1)
            rest(qs[1][:], zq[:], qs[0][:]).then_inc(S["spl_d"], 1)
            dve.wait_ge(S["sph_d"], n + 2)
            rest(ks[1][:], zk[:], ks[0][:]).then_inc(S["spl_d"], 1)
            dve.wait_ge(S["sph_d"], n + 3)
            rest(v_hl[:, :, 1, :], v_tm[:], v_hl[:, :, 0, :]).then_inc(S["spl_d"], 1)

        def cached_k_low(n, bank, c):
            dve.wait_ge(S["pj_d"], n)
            rest(kcs[1][:, 512 * c:512 * c + 512], bank[:], kcs[0][:, 512 * c:512 * c + 512]).then_inc(S["kcl_d"], 1)

        LINKS = 12

        for it in PROLOGUE_PLAN:
            if isinstance(it, str):
                if it[:2] == "KC":
                    cached_k_low(J1[it], banks[(J1[it] - 1) % 2], int(it[2]))
            elif it[0] == "FORGET":
                dve.wait_ge(S["fz_e"], 3)
                dve.tensor_scalar(fz[:], fz[:], 0.0, None, ALU.min).then_inc(S["fchain"], 1)
                dve.wait_ge(S["fchain"], 1)
                dve.tensor_tensor(logf[:], fz[:], fa[:], ALU.subtract).then_inc(S["lf_d"], 1)
                dve.wait_ge(S["lf_d"], 1)
                dve.wait_ge(S["pool1"], 1)
                dve.wait_ge(S["clT_e"], 1)
                dve.tensor_tensor_scan(csum[:, 0, 0:T_P], fones[:, 0:T_P], logf[:, 0:T_P], 0.0,
                                       ALU.mult, ALU.add).then_inc(S["csum_d"], 1)
                dve.tensor_tensor_scan(csum[:, 1, 0:PAST], fones[:, 0:PAST], clog[:], 0.0,
                                       ALU.mult, ALU.add).then_inc(S["csum_d"], 1)
                dve.wait_ge(S["csum_d"], 2)
                dve.tensor_tensor_scan(csum[:, 1, PAST:T], fones[:, PAST:T], logf[:, T_P:T],
                                       csum[:, 1, PAST - 1:PAST], ALU.mult, ALU.add).then_inc(S["csum_d"], 1)
            elif it[0] == "W" and it[1] in ("K", "V"):
                no, slot = PROLOGUE_BLOCKS[it[1]]
                w_low(slot, no)
            elif it[0] == "WFIRST":
                w_low(0, 5)
            elif it[0] == "NORM":
                invert_roots()
            elif it[0] == "SCALE":
                normalize()
            elif it[0] == "SPLIT":
                split_qkv()

        def body(U):
            u = U.u
            links = 0 if U.kind == "A" else u * LINKS - 4 * LINKS
            n_link = 0
            order = [it for it in U.plan]
            for it in order:
                if it[0] == "J" and it[1][:2] == "KC":
                    idx = U.job[it[1]]
                    cached_k_low(U.j0 + idx, banks[(idx - 1) % 2], int(it[1][2]))
                elif it[0] == "GS" and U.kind == "B":
                    dve.wait_ge(S["dst_m"], 1)
                    dve.tensor_scalar(dist[:], dist[:], 0.25, None, ALU.mult).then_inc(S["dch"], 1)
                    n_link += 1
                    dve.wait_ge(S["dch"], links + n_link)
                elif it[0] == "VC":
                    dve.wait_ge(S["vch_d"], u + 1)
                    rest(vc_hl[:, :, 1, :], vc_raw, vc_hl[:, :, 0, :]).then_inc(S["vcl_d"], 1)
                elif it[0] == "S":
                    i, m = it[1:]
                    n = keys_of(i)
                    if U.kind == "A":
                        if (i, m) == (7, 0):
                            dve.wait_ge(S["ld_cum"], u * 64 + 64)
                        term = (cum_s if i == 8 else cum_p)[m][:, 0:n]
                    else:
                        term = dist[:, 0:T] if i == 8 else dist[:, T - n:T]
                    hold(dve, "s_f", U.s0 + U.s[i, m], "hold_dve")
                    dve.tensor_tensor_reduce(out=sc[m][:, 0:n], in0=psS[:, 0:n], in1=term, scale=1.0, scalar=3e38,
                                             op0=ALU.add, op1=ALU.min, accum_out=smin[:, m:m + 1]
                                             ).then_inc(S["s_d"], 1)
                elif it[0] == "C":
                    i, n = it[1], keys_of(it[1])
                    c = U.grp[i, 0]
                    dve.wait_ge(S["p_d"], U.s0 + U.s[i, 1])
                    dve.reciprocal(inv0[:, i:i + 1], den[:, 0:1])
                    dve.reciprocal(rden[:, 1:2], den[:, 1:2]).then_inc(S["dch"], 1)
                    n_link += 1
                    dve.wait_ge(S["dch"], links + n_link)
                    dve.scalar_tensor_tensor(rden[:, 0:1], rden[:, 1:2], neg_lam, den[:, 0:1],
                                             ALU.mult, ALU.mult).then_inc(S["rd_d"], 1)
                    dve.wait_ge(S["rd_d"], 72 + c + (u * 9 - 36))
                    dve.scalar_tensor_tensor(sc[0][:, 0:n], sc[1][:, 0:n], rden[:, 0:1], sc[0][:, 0:n],
                                             ALU.mult, ALU.add).then_inc(S["cb_d"], 1)
                elif it[0] == "T":
                    i, m = it[1:]
                    g = U.g0 + U.grp[i, m]
                    dve.wait_ge(S["th_d"], g)
                    nb = 8 if i == 8 else i + 1
                    r = rest(pt[1][:, 0:nb, :], psT[:, 0:P * nb].rearrange("p (t c) -> p t c", c=P), pt[0][:, 0:nb, :])
                    if i == 8:
                        r = rest(pt[1][0:T_S, 8, :], psO[0:T_S, 256:384], pt[0][0:T_S, 8, :])
                    r.then_inc(S["tl_d"], 1)
                    if U.kind == "A":
                        dve.reciprocal(rden[:, m:m + 1], den[:, m:m + 1]).then_inc(S["rd_d"], 1)
                elif it[0] == "AV":
                    i, m = it[1:]
                    g = U.g0 + U.grp[i, m]
                    dve.wait_ge(S["av_f"], g)
                    if U.grp[i, m] == 1 and (not isinstance(u, int) or u > 0):
                        dve.wait_ge(S["pj_f"], U.j0)
                    w = DH if U.kind == "A" else P
                    dve.tensor_reduce(out=o_tm[:, i, w * m:w * m + w], in_=psO[:, 0:2 * w].rearrange("p (a d) -> p d a", a=2),
                                      axis=AX, op=ALU.add).then_inc(S["o_d"], 1)
                elif it[0] == "L":
                    w_low(SLOT[it[1]], U.block(it[1]))
                elif it[0] == "RD":
                    invert_roots(U)
                elif it[0] == "SCALE":
                    normalize(U)
                elif it[0] == "SPLIT":
                    split_qkv(U)
                elif it[0] == "OFIN" and U.kind == "B":
                    dve.wait_ge(S["rs_d"], u - 3)
                    dve.reciprocal(rsub, rsub).then_inc(S["dch"], 1)
                    dve.wait_ge(S["dch"], links + n_link + 1)
                    dve.tensor_tensor(rsub, rsub, inv0[:], ALU.mult).then_inc(S["dch"], 1)
                    n_link += 2
                    dve.wait_ge(S["dch"], links + n_link)
                    dve.tensor_tensor(o_tm[:], o_tm[:], rsub.rearrange("p (t a) -> p t a", a=1).broadcast_to([P, NT, P]),
                                      ALU.mult).then_inc(S["of_d"], 1)
            assert not U.nxt or n_link == (0 if U.kind == "A" else LINKS)

        units(dve, body)

        def w3_low(s, number):
            dve.wait_ge(S["w3h"], number)
            rest(wsp3[s][1][:], wraw3[s][:], wsp3[s][0][:]).then_inc(S["w3l"], 1)

        w3_low(0, 1)
        w3_low(1, 2)
        for k in range(UNITS):
            dve.wait_ge(S["oh_d"], k + 1)
            rest(os_[1][:, k, :], o_all[:, k, :], os_[0][:, k, :]).then_inc(S["ol_d"], 1)

        def merge(i):
            for s in range(2):
                for c, (c0, m) in enumerate(CHUNKS):
                    j, x = i * 6 + (3 * s + c), (3 * s + c) % 2
                    if c == 0:
                        dve.wait_ge(S["ld_g"], i * 64 + (32 * s + 32))
                    dve.wait_ge(S["mg_f"], j + 1)
                    for g, bank in ((0, psS), (1, psT)):
                        r = dve.scalar_tensor_tensor(mt[x][g][:, 0:m], gates[g][:, c0:c0 + m], 1.0,
                                                     bank[:, 512 * x:512 * x + m], ALU.add, ALU.mult)
                    r.then_inc(S["gmul"], 1)
                    dve.wait_ge(S["gmul"], j + 1)
                    dve.tensor_tensor(mt[x][0][:, 0:m], mt[x][0][:, 0:m], mt[x][1][:, 0:m], ALU.add).then_inc(S["mg_d"], 1)
                    dve.wait_ge(S["m_h"], j + 1)
                    dve.scalar_tensor_tensor(ms[1][:, i * 2 + s, c0:c0 + m], mt[x][0][:, 0:m], 0.5,
                                             high_of(ms[0][:, i * 2 + s, c0:c0 + m]), ALU.mult, ALU.subtract
                                             ).then_inc(S["m_l"], 1)
                w3_low(s, i * 2 + (s + 3))

        with dve.Fori(0, 4) as i:
            merge(i)

        for fb in range(KB):
            for c, (c0, m) in enumerate(CHUNKS):
                j = 3 * fb + c
                dve.wait_ge(S["wo_f"], j + 1)
                if c == 0:
                    dve.wait_ge(S[f"ld_xi{fb % 2}"], 16 * (fb // 2 + 1))
                dve.tensor_tensor(x1[:, fb, c0:c0 + m], banks[j % 2][:, 0:m], x_in[fb % 2][:, c0:c0 + m],
                                  ALU.add).then_inc(S["x1_d"], 1)
            w3_low(fb % 2, KB + 2 + fb + 1)
        dve.wait_ge(S["sqrt4"], 3)
        link(dve.reciprocal(rstd4[:], rstd4[:]))
        dve.wait_ge(S["x1_d"], 3 * KB)

        def x2_scaled(k):
            wait(dve, "x2l", k - 1)
            dve.scalar_tensor_tensor(sq4[k % 2][:], x1[:, k, :], gain_ffn[:, k:k + 1], rstd4[:],
                                     ALU.mult, ALU.mult).then_inc(S["t4_s"], 1)

        def x2_low(k):
            dve.wait_ge(S["x2h"], k + 1)
            rest(x2s[1][:, k, :], sq4[k % 2][:], x2s[0][:, k, :]).then_inc(S["x2l"], 1)

        x2_scaled(0)
        for k in range(1, KB):
            x2_scaled(k)
            x2_low(k - 1)
        x2_low(KB - 1)
        for h in range(2):
            dve.memset(ub[h][:, 0:2], 0.0).then_inc(S["pads"], 1)
            dve.memset(ct[h][:, 0:2], 0.0).then_inc(S["pads"], 1)
        dve.sem_inc(S["u_free"], 2)
        dve.sem_inc(S["gl_free"], 1)
        dve.sem_inc(S["dn_free"], 3)
        blk, f0 = 2 * KB, 0
        for gi, ng in enumerate(GROUPS):
            with dve.Fori(0, ng) as i:
                for h in range(2):
                    b = i + (f0 + FB * h)
                    dve.wait_ge(S["ct_a"], i * 2 + (2 * f0 + h + 1))
                    dve.scalar_tensor_tensor(ct[h][:], ub[h][:, 1:TU - 1], taps[1][:, bass.ds(b, 1)], ct[h][:],
                                             ALU.mult, ALU.add).then_inc(S["c1_d"], 1)
                    gap = TU - 2 - T_P
                    dve.tensor_copy(edges[:, :, b].rearrange("p (a r) -> p a r", r=2),
                                    ub[h][:, T_P:T_P + 2 * gap].rearrange("p (a r) -> p a r", r=gap)[:, :, 0:2]
                                    ).then_inc(S["edge_d"], 1)
                    dve.wait_ge(S["c1_d"], i * 2 + (2 * f0 + h + 1))
                    dve.scalar_tensor_tensor(ct[h][:], ub[h][:, 0:TU - 2], taps[0][:, bass.ds(b, 1)], ct[h][:],
                                             ALU.mult, ALU.add).then_inc(S["u_free"], 1)
                    dve.wait_ge(S["w3h"], i * 2 + (blk + 3 + h))
                    rest(wsp3[h][1][:], wraw3[h][:], wsp3[h][0][:]).then_inc(S["w3l"], 1)
                dve.wait_ge(S["silu_d"], i + (f0 + 1))
                dve.wait_ge(S["u_free"], i * 2 + (2 * f0 + 4))
                dve.tensor_tensor(ct[1][:], ct[0][:], ct[1][:], ALU.mult).then_inc(S["gm_d"], 1)
                dve.wait_ge(S["gh_d"], i + (f0 + 1))
                rest(gsp[1][:, i, 0:T_P], ct[1][:, 0:T_P], gsp[0][:, i, 0:T_P])
                rest(gsp[1][:, i, T_P:T], ct[1][:, T_P + 2:TU - 2], gsp[0][:, i, T_P:T]).then_inc(S["gl_free"], 1)
            f0 += ng
            blk += 2 * ng
            final = gi == len(GROUPS) - 1

            def down(i):
                for s in range(2):
                    for c, (c0, m) in enumerate(CHUNKS):
                        x = 3 * s + c
                        dve.wait_ge(S["dn_f"], i * 6 + (24 * gi + x + 1))
                        now = x1[:, i * 2 + s, c0:c0 + m]
                        out = y_blk[s][:, c0:c0 + m] if final else now
                        dve.tensor_tensor(out, ring_d[x % 3][:, 0:m], now, ALU.add).then_inc(S["dn_free"], 1)
                    if not (final and isinstance(i, int)):
                        dve.wait_ge(S["w3h"], i * 2 + (blk + 3 + s))
                        rest(wsp3[s][1][:], wraw3[s][:], wsp3[s][0][:]).then_inc(S["w3l"], 1)

            if final:
                with dve.Fori(0, 3) as i:
                    down(i)
                down(3)
            else:
                with dve.Fori(0, 4) as i:
                    down(i)
            blk += 8

    ctx.close()


_INS = ["x_prompt", "x_sample", "cache_a_k", "cache_a_v", "cache_a_logf", "cache_b_k", "cache_b_v",
        "state_ffn_conv", "g_attn", "w_in", "b_f", "qn_a", "kn_a", "qn_b", "kn_b",
        "lambda_q1", "lambda_k1", "lambda_q2", "lambda_k2", "subln_b", "w_oa", "w_ob", "w_out",
        "g_ffn", "w_up", "conv_w", "conv_b", "w_down"]
_OUTS = [(1, T_P, D), (1, T_S, D),
         (1, T_P, 8, 64), (1, T_P, 8, 64), (1, T_P, 8), (1, T_P, 4, 2, 64), (1, T_P, 4, 128), (1, 2, 2 * D_FF),
         (1, T_S, 8, 64), (1, T_S, 8, 64), (1, T_S, 8), (1, T_S, 4, 2, 64), (1, T_S, 4, 128), (1, 2, 2 * D_FF)]


def kernel(**inputs):
    import numpy as _np
    import concourse.bacc as _bacc
    from concourse import mybir as _mybir
    from concourse.bass_utils import run_bass_kernel_spmd as _run

    nc = _bacc.Bacc("TRN2", target_bir_lowering=False, num_devices=1)
    arrays, ins, outs = {}, [], []
    for name in _INS:
        a = _np.ascontiguousarray(inputs[name])
        arrays[f"in_{name}"] = a
        ins.append(nc.dram_tensor(f"in_{name}", a.shape, _mybir.dt.from_np(a.dtype), kind="ExternalInput").ap())
    for i, shape in enumerate(_OUTS):
        outs.append(nc.dram_tensor(f"out_{i}", shape, _mybir.dt.float32, kind="ExternalOutput").ap())
    build(nc, ins, outs)
    r = _run(nc, [arrays], core_ids=[0])
    return tuple(r.results[0][f"out_{i}"] for i in range(len(_OUTS)))
```

```python
import math
from contextlib import ExitStack

import concourse.bass as bass
from concourse import mybir

F32 = mybir.dt.float32
F32R = mybir.dt.float32r
I32 = mybir.dt.int32
ALU = mybir.AluOpType
ACT = mybir.ActivationFunctionType
AX = mybir.AxisListType.X

P = 128
D = 1024
T_P = 1024
T_S = 64
T = T_P + T_S
PAST = 1024
KB = D // P
DH = 64
H_A = 8
W_A = 512
W_B = 512
D_FF = 2816
FB = D_FF // P
EPS = 1e-6
LAMBDA_INIT = 0.8 - 0.6 * math.exp(-0.3 * (1 - 1))
BIG = 2.0 ** 100
NT = 9
CHUNKS = [(0, 364), (364, 364), (728, 360)]
Z_QA, Z_KA, Z_VA, Z_F = 0, W_A, 2 * W_A, 3 * W_A
Z_QB = 3 * W_A + H_A
Z_KB, Z_VB = Z_QB + W_B, Z_QB + 2 * W_B
Z_G = Z_QB + 3 * W_B
UNITS = 8
TILES = [7, 8, 6, 5, 4, 3, 2, 1, 0]
GROUPS = [6, 6, 5, 5]
PASSES = [(0, 0), (0, 1), (1, 0)]

PROLOGUE_PLAN = ["F0", "F1", "F2", ("W", "K"), "Q0", "Q1", "Q2", ("FORGET",), ("W", "V"), "K0", "K1", "K2",
                 "KC0", "KC1", "SS0", "SS1", ("NORM",), "V0", "NQ0", "NQ1", "NQ2", "NK0", "NK1", "NK2", ("SCALE",),
                 "V1", "KT0", "KT1", "KT2", ("SPLIT", 0, 1), "V2", "VT0", "VT1", "VT2", ("WFIRST",), ("SPLIT", 2)]
PROLOGUE_JOBS = [x for x in PROLOGUE_PLAN if isinstance(x, str)]
PROLOGUE_BLOCKS = {"F": (1, 1), "Q": (2, 0), "K": (3, 1), "V": (4, 0)}


def unit_plan(kind, nxt):
    if kind == "A":
        gaps = {-1: [["Q0"], ["Q1"]], 7: [["Q2"], ["SS0", "K0"]], 8: [["K1"], ["K2", "V0"]],
                6: [["SS1"], ["V1"]], 5: [["V2"], ["NQ0", "VT0"]], 4: [["NQ1", "VT1"], ["VT2", "NQ2"]],
                3: [["G00"], ["NK0", "NK1"]], 2: [["NK2", "KC0"], ["G01"]], 1: [["KT0", "KT1"], ["G02"]],
                0: [["KT2", "KC1", "/G10"], ["G10"]]}
    elif nxt:
        gaps = {-1: [["Q0"], ["Q1"]], 7: [[], ["Q2", "K0"]], 8: [["SS0", "KC0"], ["K1"]],
                6: [["K2"], ["SS1", "V0"]], 5: [["V1"], ["V2"]], 4: [["VT0", "VT1"], ["VT2", "G00"]],
                3: [["NQ0", "NQ1"], ["G01", "NQ2"]], 2: [["NK0"], ["G02"]], 1: [["NK1", "NK2"], ["G10"]],
                0: [["KT0", "KT1"], ["KT2", "KC1"]]}
    else:
        gaps = {-1: [["G00"], []], 7: [[], ["G01"]], 8: [["/G02"], ["G02"]], 6: [[], ["G10"]], 5: [[], ["G11"]],
                4: [[], ["G12"]], 3: [[], []], 2: [[], []], 1: [[], []], 0: [[], []]}
    end = ["SPLIT", "G11", "G12", "OT0", "OT1", "OT2"] if nxt else ["OT0", "OT1", "OT2"]
    then = {"SS1": [("ROOT",)], **({"G02": [("H", "FIRST")]} if nxt else {}),
            **{a: [("H", b)] for a, b in WEIGHTS_AFTER[nxt].items()}}
    later = {"SS1": [("RD",)], "NK2": [("SCALE",)], **({"G02": [("L", "FIRST")]} if nxt else {}),
             **{a: [("L", b)] for a, b in WEIGHTS_AFTER[nxt].items()}}
    pending = []
    plan = [("GS",)]

    def jobs(names):
        for n in names:
            if n == "SPLIT":
                plan.append((n,))
            elif n[0] == "/":
                plan.append(("HALF", n[1:]))
            else:
                plan.append(("J", n))
                plan.extend(then.get(n, []))
                pending.extend(later.get(n, []))

    def flush():
        plan.extend(pending)
        pending.clear()

    plan.append(("S", 7, 0))
    jobs(gaps[-1][0])
    plan.append(("S", 7, 1))
    jobs(gaps[-1][1])
    flush()
    if kind == "B":
        plan.append(("C", 7))
    for n, i in enumerate(TILES):
        after = TILES[n + 1] if n + 1 < NT else None
        g = gaps[i]
        plan.append(("T", i, 0))
        if after is not None:
            plan.append(("S", after, 0))
        jobs(g[0])
        plan.append(("AV", i, 0))
        flush()
        if i == TILES[0]:
            plan.append(("VC",))
        if kind == "A":
            plan.append(("T", i, 1))
        if after is not None:
            plan.append(("S", after, 1))
        jobs(g[1])
        if kind == "A":
            plan.append(("AV", i, 1))
            flush()
        elif after is not None:
            plan.append(("C", after))
    plan.append(("OFIN",))
    flush()
    jobs(end)
    assert not pending
    return plan


WEIGHTS_AFTER = {True: {"Q0": "K", "K0": "V", "V2": "G0", "G00": "G1"}, False: {"G00": "G1"}}
BLOCKS = {True: ["Q", "K", "V", "G0", "G1"], False: ["G0", "G1"]}
SLOT = {"FIRST": 0, "Q": 0, "K": 1, "V": 0, "G0": 0, "G1": 1}


def plan_index(plan):
    job, s, grp = {}, {}, {}
    for it in plan:
        if it[0] == "J":
            job[it[1]] = len(job) + 1
        elif it[0] == "S":
            s[it[1:]] = len(s) + 1
        elif it[0] == "T":
            grp[it[1:]] = len(grp) + 1
    return job, s, grp


def keys_of(i):
    return PAST + T_S if i == 8 else P * (i + 1)


def build(nc, ins, outs):
    ctx = ExitStack()
    sem = lambda n: ctx.enter_context(nc.semaphore(n))

    (x_p, x_s, c_ak, c_av, c_alogf, c_bk, c_bv, st_conv, g_attn, w_in, b_f, qn_a, kn_a, qn_b, kn_b,
     l_q1, l_k1, l_q2, l_k2, subln, w_oa, w_ob, w_out, g_ffn, w_up, conv_w, conv_b, w_down) = ins
    (y_p, y_s, p_ak, p_av, p_alogf, p_bk, p_bv, p_conv, s_ak, s_av, s_alogf, s_bk, s_bv, s_conv) = outs
    w_in_v = w_in.rearrange("(k p) n -> p k n", p=P)
    def heads(a, tiles):
        if len(a.shape) == 5:
            return a.rearrange("o (t p) u m d -> u (o p) t (m d)", t=tiles)
        if a.shape[3] == P:
            return a.rearrange("o (t p) u d -> u (o p) t d", t=tiles)
        return a.rearrange("o (t p) (u h) d -> u (o p) t (h d)", t=tiles, h=2)

    x_scr = nc.dram_tensor("x_scr", (KB, P, T), F32).ap()
    gate_scr = nc.dram_tensor("gate_scr", (16, P, T), F32).ap()
    o_scr = nc.dram_tensor("o_scr", (UNITS - 1, P, T), F32).ap()
    c_scr = nc.dram_tensor("c_scr", (2, H_A, T), F32).ap()

    def alloc(stack):
        return (lambda n, s, d=F32: stack.enter_context(nc.sbuf_tensor(n, s, d)),
                lambda n, s: stack.enter_context(nc.psum_tensor(n, s, F32)))

    sb, pb = alloc(ctx)
    ident = sb("ident", [P, P])
    vecs = sb("vecs", [P, 6 * 44 + 16])
    taps = [vecs[:, 44 * i:44 * i + 44] for i in range(3)]
    cbias = vecs[:, 132:176]
    cstate = vecs[:, 176:264]
    gain_attn, gain_ffn = vecs[:, 264:272], vecs[:, 272:280]
    small = sb("small", [P, 48])
    eps_t = small[:, 0:1]
    gq_a, gk_a, gq_b, gk_b = (small[:, i:i + 1] for i in range(1, 5))
    sub_g = small[:, 5:6]
    neg_lam = small[:, 6:7]
    den = small[:, 8:10]
    rden = small[:, 10:12]
    smin = small[:, 12:14]
    sumsq = small[:, 16:25]
    rsub = small[:, 26:35]
    meansq = sb("meansq", [P, NT, 2, 2])
    root = sb("root", [P, NT, 2, 2])
    inv0 = sb("inv0", [P, NT])
    bf_t = small[0:H_A, 36:37]
    one_t = small[:, 40:41]
    xact = ExitStack()

    banks = [pb(f"bank{i}", [P, 512]) for i in range(2)]
    psS = pb("psS", [P, 3 * 512])
    psT = pb("psT", [P, 2 * 512])
    psO = pb("psO", [P, 512])
    TGROUPS = [range(0, 3), range(3, 6), range(6, 9)]
    ring_u = [banks[0], banks[1], psS[:, 0:512], psS[:, 512:1024], psS[:, 1024:1536], psO]
    ring_d = [banks[0], banks[1], psO]
    first6 = [banks[0], banks[1], psS[:, 0:512], psS[:, 512:1024], psS[:, 1024:1536], psO]
    three = [psS[:, 512 * c:512 * c + CHUNKS[c][1]] for c in range(3)]

    sb_n, _ = alloc(xact)
    xn = [sb_n("xn_hi", [P, KB, T], F32R), sb_n("xn_lo", [P, KB, T], F32R)]
    wraw = sb_n("wraw", [P, KB, P])
    wsp = [[sb_n(f"w_{'hl'[h]}{s}", [P, KB, P], F32R) for h in range(2)] for s in range(2)]
    ident_r = sb_n("ident_r", [P, P], F32R)
    mask_r = sb_n("mask_r", [P, P], F32R)
    half_ones = sb_n("half_ones", [P, P])

    s1 = ExitStack()
    sb1, _ = alloc(s1)
    x_tm = sb1("x_tm", [P, NT, D])
    xT = sb1("xT", [P, KB, T])
    sq1 = [sb1(f"sq1_{i}", [P, T]) for i in range(2)]
    rstd1 = sb1("rstd1", [P, T])
    rows = sb1("rows", [44, 8, P])
    all_ones = sb1("all_ones", [P, P])
    lamv = sb1("lamv", [P, 4, DH])
    lamt = sb1("lamt", [P, 2 * DH + 4])
    maskf = sb1("maskf", [P, P])
    clog_tm = sb1("clog_tm", [P, 8, H_A])
    clog = sb1("clog", [H_A, PAST])
    s1.close()
    s1b = ExitStack()
    sb1b, _ = alloc(s1b)
    fz = sb1b("fz", [H_A, T])
    fa = sb1b("fa", [H_A, T])
    fones = sb1b("fones", [H_A, T])
    logf = sb1b("logf", [H_A, T])
    csum = sb1b("csum", [H_A, 2, T])
    lf_tm = sb1b("lf_tm", [P, NT, H_A])
    s1b.close()

    s2 = ExitStack()
    sb2, _ = alloc(s2)
    qs = [sb2(f"q_{'hl'[h]}", [P, T], F32R) for h in range(2)]
    ks = [sb2(f"k_{'hl'[h]}", [P, T], F32R) for h in range(2)]
    v_hl = sb2("v_hl", [P, NT, 2, P], F32R)
    kcs = [sb2(f"kc_{'hl'[h]}", [P, PAST], F32R) for h in range(2)]
    vc_hl = sb2("vc_hl", [P, 8, 2, P], F32R)
    zq, zk, zv = (sb2(n, [P, T]) for n in ("zq", "zk", "zv"))
    sqq, sqk = (sb2(n, [P, T]) for n in ("sqq", "sqk"))
    v_tm = sb2("v_tm", [P, NT, P])
    k_tm = sb2("k_tm", [P, NT, P])
    kc_tm = sb2("kc_tm", [P, 8, P])
    o_tm = sb2("o_tm", [P, NT, P])
    junk = sb2("junk", [P, P])
    sc = [sb2(f"sc{m}", [P, T]) for m in range(2)]
    pt = [sb2(f"pT_{'hl'[h]}", [P, NT, P], F32R) for h in range(2)]
    cum_p = [sb2(f"cum_p{m}", [P, T_P]) for m in range(2)]
    cum_s = [sb2(f"cum_s{m}", [P, T]) for m in range(2)]
    dist, dist_i = cum_s[0][:], cum_s[1][:].bitcast(I32)
    vc_raw = sqk[:, 0:PAST].rearrange("p (t c) -> p t c", c=P)
    gate_st = [zv, sqq]
    oT_st = sqk
    s2.close()
    xact.close()

    s3 = ExitStack()
    sb3, _ = alloc(s3)
    wraw3 = [sb3(f"wraw3_{s}", [P, KB, P]) for s in range(2)]
    wsp3 = [[sb3(f"w3_{'hl'[h]}{s}", [P, KB, P], F32R) for h in range(2)] for s in range(2)]
    s3r = ExitStack()
    sb3r, _ = alloc(s3r)
    o_all = sb3r("o_all", [P, UNITS, T])
    s3r.close()
    s3m = ExitStack()
    sb3m, _ = alloc(s3m)
    ms = [sb3m(f"m_{'hl'[h]}", [P, KB, T], F32R) for h in range(2)]
    s3o = ExitStack()
    sb3o, _ = alloc(s3o)
    os_ = [sb3o(f"o_{'hl'[h]}", [P, KB, T], F32R) for h in range(2)]
    gates = [sb3o(f"gate{i}", [P, T]) for i in range(2)]
    mt = [[sb3o(f"m_{'ab'[g]}{x}", [P, 364]) for g in range(2)] for x in range(2)]
    s3o.close()
    s4 = ExitStack()
    sb4, _ = alloc(s4)
    x1 = sb4("x1", [P, KB, T])
    rstd4 = sb4("rstd4", [P, T])
    ones4 = sb4("ones4", [P, P])
    x_in = [sb4(f"x_in{i}", [P, T]) for i in range(2)]
    ones_r = sb4("ones_r", [P, P], F32R)
    sq4 = [sb4(f"sq4_{i}", [P, T]) for i in range(2)]
    sq4s = [[sb4(f"sq4_{'hl'[h]}{i}", [P, T], F32R) for h in range(2)] for i in range(2)]
    sums_out = [psT[:, 0:CHUNKS[0][1]], psT[:, 512:512 + CHUNKS[1][1]], psO[:, 0:CHUNKS[2][1]]]
    s4.close()
    s3m.close()
    s5 = ExitStack()
    sb5, _ = alloc(s5)
    x2s = [sb5(f"x2_{'hl'[h]}", [P, KB, T], F32R) for h in range(2)]
    sb5("x1_stays", [P, KB, T])
    sb5("rstd4_stays", [P, T])
    gsp = [sb5(f"g_{'hl'[h]}", [P, max(GROUPS), T], F32R) for h in range(2)]
    TU = T + 4
    ub = [sb5(f"u{i}", [P, NT * P + 8]) for i in range(2)]
    edges = sb5("edges", [P, 4, 2 * FB])
    edge_rows = sb5("edge_rows", [4 * FB, 2, P])
    ct = [sb5(f"ct{i}", [P, TU - 2]) for i in range(2)]
    y_blk = [c[:, 0:T] for c in ct]
    y_tm = [u[:, 0:NT * P].rearrange("p (t c) -> p t c", c=P) for u in ub]
    s5.close()
    s3.close()

    names = ("ld_vec ld_x0 ld_x1 ld_xs ld_small ld_clog lf_out c_out x_out "
             "idt cst dst msk vecT vecD xT_f xT_e sq_d ms_f sqrt1 xh_s xl_s xh_d pool1 "
             "fz_e fchain lf_d csum_d clT_f clT_e lfT_f lfT_e lam_v lam_a small_d vpad "
             "wraw_s wh_d wl_d pj_f pj_d kcl_d s_f s_d p_d rd_d cb_d t_f th_d tl_d av_f o_d om_d "
             "rs_d of_d sq_rt rt_d norm_d sph_d spl_d vch_d vcl_d dch st_v st_k st_g0 st_g1 st_o ld_vc ld_kc ld_cum "
             "w3_s0 w3_s1 w3h w3l ld_o oh_d ol_d mg_f mg_d ld_g gmul m_h m_l ld_xi0 ld_xi1 wo_f x1_d sq4_d sq4h sq4l "
             "ms4_f sqrt4 x2h x2l on4 ones_d up_f up_free u_free edge_d edge_o edgeT_f edgeT_e ct_a c1_d silu_d gm_d gh_d gl_free dn_f dn_free "
             "dst_a dst_m idr ms_pad hold_pe state_d yT_f yT_free y_o0 y_o1 pads hold_dve hold_pool dchain").split()
    S = {n: sem(n) for n in names}

    def wait(e, name, value):
        if isinstance(value, int) and value <= 0:
            return
        e.wait_ge(S[name], value)

    def hold(e, name, value, own):
        if isinstance(value, int) and value <= 0:
            return
        e.wait_ge(S[name], value)
        e.sem_inc(S[own], 1)

    PLANS = {(k, n): unit_plan(k, n) for k, n in (("A", True), ("B", True), ("B", False))}
    INDEX = {kn: plan_index(p) for kn, p in PLANS.items()}
    JOBS1 = PROLOGUE_JOBS
    J_PRO, J_UNIT = len(JOBS1), len(INDEX["A", True][0])
    assert J_PRO % 2 == 0 and J_UNIT % 2 == 0 and J_UNIT == len(INDEX["B", True][0])
    J1 = {n: i + 1 for i, n in enumerate(JOBS1)}

    class Unit:
        def __init__(self, u, kind, nxt):
            self.u, self.kind, self.nxt = u, kind, nxt
            self.plan = PLANS[kind, nxt]
            self.job, self.s, self.grp = INDEX[kind, nxt]
            self.next_kind = None if not nxt else ("B" if kind == "B" or (isinstance(u, int) and u == 3) else "A")
            self.j0 = u * J_UNIT + J_PRO
            self.w0 = u * 5 + 4
            self.s0 = u * 18
            self.g0 = u * 18 if kind == "A" else u * 9 + 36

        def block(self, name):
            return self.w0 + (6 if name == "FIRST" else BLOCKS[self.nxt].index(name) + 1)

    def units(e, body):
        with e.Fori(0, 3) as u:
            body(Unit(u, "A", True))
        body(Unit(3, "A", True))
        with e.Fori(4, 7) as u:
            body(Unit(u, "B", True))
        body(Unit(7, "B", False))

    block = ctx.enter_context(nc.Block())

    @block.sync
    def _(sp):
        sp.dma_start(x_tm[0:T_S, 8, :], x_s[0]).then_inc(S["ld_xs"], 16)
        for h in range(2):
            half = slice(D // 2 * h, D // 2 * (h + 1))
            sp.dma_start(x_tm[:, 0:8, half], x_p.rearrange("o (t p) d -> (o p) t d", p=P)[:, :, half]
                         ).then_inc(S[f"ld_x{h}"], 16)

        def load_w(dst, b, src):
            wait(sp, "wl_d", b - 1)
            sp.dma_start(dst, src).then_inc(S["wraw_s"], 16)

        for n, c in enumerate([Z_F, Z_QA, Z_KA, Z_VA]):
            load_w(wraw[:], n + 1, w_in_v[:, :, c:c + P])

        def cols(base, first, u):
            if isinstance(u, int):
                at = base + (u - first) * P
                return w_in_v[:, :, at:at + P]
            lo = base - first * P
            view = w_in_v[:, :, lo % P:lo % P + (5128 - lo % P) // P * P].rearrange("p k (u c) -> u p k c", c=P)
            return view[u + lo // P]

        def body(U):
            if U.nxt:
                to_b = U.next_kind == "B"
                for base in ([Z_QB, Z_KB, Z_VB] if to_b else [Z_QA, Z_KA, Z_VA]):
                    load_w(wraw[:], U.block("QKV"[[Z_QB, Z_KB, Z_VB, Z_QA, Z_KA, Z_VA].index(base) % 3]),
                           cols(base, 4 if to_b else 0, U.u + 1))
            gv = w_in_v[:, :, Z_G:].rearrange("p k (u g c) -> u g p k c", g=2, c=P)
            for g in range(2):
                load_w(wraw[:], U.block(f"G{g}"), gv[U.u][g])

        units(sp, body)

        wait(sp, "pj_f", J_PRO + 7 * J_UNIT + INDEX["B", False][0]["G12"])
        oa = w_oa.rearrange("(k p) (i s c) -> i s p k c", p=P, c=P, s=2)
        ob = w_ob.rearrange("(k p) (i s c) -> i s p k c", p=P, c=P, s=2)
        wo = w_out.rearrange("(k p) (i s c) -> i s p k c", p=P, c=P, s=2)
        for s in range(2):
            sp.dma_start(wraw3[s][:, 0:4, :], oa[0][s]).then_inc(S[f"w3_s{s}"], 16)
            sp.dma_start(wraw3[s][:, 4:8, :], ob[0][s]).then_inc(S[f"w3_s{s}"], 16)
        with sp.Fori(1, 4) as i:
            for s in range(2):
                sp.wait_ge(S["w3l"], i * 2 + (s - 1))
                sp.dma_start(wraw3[s][:, 0:4, :], oa[i][s]).then_inc(S[f"w3_s{s}"], 16)
                sp.dma_start(wraw3[s][:, 4:8, :], ob[i][s]).then_inc(S[f"w3_s{s}"], 16)
        with sp.Fori(4, 8) as i:
            for s in range(2):
                sp.wait_ge(S["w3l"], i * 2 + (s - 1))
                sp.dma_start(wraw3[s][:], wo[i - 4][s]).then_inc(S[f"w3_s{s}"], 16)
        base, f0 = 8, 0
        up = w_up.rearrange("(k p) (h j c) -> j h p k c", p=P, c=P, h=2)
        dn = w_down.rearrange("(k p) (i s c) -> i s p k c", p=P, c=P, s=2)
        for ng in GROUPS:
            with sp.Fori(0, ng) as i:
                for s in range(2):
                    sp.wait_ge(S["w3l"], i * 2 + (2 * base + s - 1))
                    sp.dma_start(wraw3[s][:], up[i + f0][s]).then_inc(S[f"w3_s{s}"], 16)
            base += ng
            with sp.Fori(0, 4) as i:
                for s in range(2):
                    sp.wait_ge(S["w3l"], i * 2 + (2 * base + s - 1))
                    sp.dma_start(wraw3[s][:, 0:ng, :], dn[i][s][:, f0:f0 + ng, :]).then_inc(S[f"w3_s{s}"], 16)
            base += 4
            f0 += ng

    @block.gpsimd
    def _(pool):
        pool.memset(ident[:], 0.0).then_inc(S["idt"], 1)
        pool.wait_ge(S["idt"], 1)
        pool.affine_select(out=ident[:], in_=ident[:], compare_op=ALU.not_equal, fill=1.0, base=0,
                           pattern=[[-1, P]], channel_multiplier=1).then_inc(S["idt"], 1)
        pool.memset(all_ones[:], 1.0 / D).then_inc(S["cst"], 1)
        pool.memset(eps_t, EPS).then_inc(S["cst"], 1)
        pool.memset(half_ones[:], 0.0).then_inc(S["cst"], 1)
        pool.wait_ge(S["cst"], 3)
        pool.memset(half_ones[0:DH, 0:DH], 1.0 / DH).then_inc(S["cst"], 1)
        pool.memset(half_ones[DH:P, DH:P], 1.0 / DH).then_inc(S["cst"], 1)
        pool.wait_ge(S["cst"], 5)
        pool.memset(maskf[:], 0.0).then_inc(S["msk"], 1)
        pool.wait_ge(S["msk"], 1)
        pool.affine_select(out=maskf[:], in_=maskf[:], compare_op=ALU.is_ge, fill=BIG, base=0,
                           pattern=[[-1, P]], channel_multiplier=1).then_inc(S["msk"], 1)
        for i in range(6):
            src = [conv_w[0], conv_w[1], conv_w[2], conv_b, st_conv[0, 0], st_conv[0, 1]][i]
            pool.dma_start(rows[:, i, :], src.rearrange("(b c) -> b c", c=P)).then_inc(S["ld_vec"], 16)
        for i, g in ((6, g_attn), (7, g_ffn)):
            pool.dma_start(rows[0:KB, i, :], g.rearrange("(b c) -> b c", c=P)).then_inc(S["ld_vec"], 16)
        for i, g in enumerate((qn_a, kn_a, qn_b, kn_b)):
            for h in range(2):
                pool.dma_start(small[DH * h:DH * h + DH, 1 + i:2 + i],
                               g.rearrange("(p a) -> p a", a=1)).then_inc(S["ld_small"], 16)
        pool.dma_start(sub_g, subln.rearrange("(p a) -> p a", a=1)).then_inc(S["ld_small"], 16)
        pool.dma_start(bf_t, b_f.rearrange("(p a) -> p a", a=1)).then_inc(S["ld_small"], 16)
        for i, l in enumerate((l_q1, l_k1, l_q2, l_k2)):
            pool.dma_start(lamv[:, i, :], l.rearrange("(a d) -> a d", a=1).broadcast_to([P, DH])).then_inc(S["ld_small"], 16)
        pool.dma_start(clog_tm[:], c_alogf.rearrange("o (t p) h -> (o p) t h", p=P)).then_inc(S["ld_clog"], 16)
        for k in range(KB):
            pool.wait_ge(S["xT_e"], 3 * k + 3)
            pool.dma_start(x_scr[k], xT[:, k, :]).then_inc(S["x_out"], 16)

        def store_kv(which, to, un, tile, count):
            hold(pool, "pj_d", count, "hold_pool")
            a, b = {("A", "v"): (p_av, s_av), ("A", "k"): (p_ak, s_ak),
                    ("B", "v"): (p_bv, s_bv), ("B", "k"): (p_bk, s_bk)}[to, which]
            pool.dma_start(heads(a, 8)[un], tile[:, 0:8, :]).then_inc(S["st_" + which], 16)
            pool.dma_start(heads(b, 1)[un], tile[0:T_S, 8:9, :]).then_inc(S["st_" + which], 16)

        def load_kc(to, un):
            pool.dma_start(kc_tm[:], heads(c_ak if to == "A" else c_bk, 8)[un]).then_inc(S["ld_kc"], 16)

        def load_cum(un):
            for m in range(2):
                cu = lambda a: c_scr[a].rearrange("(u m) t -> u m t", m=2)[un][m:m + 1, :]
                pool.dma_start(cum_p[m][:], cu(0)[:, 0:T_P].broadcast_to([P, T_P])).then_inc(S["ld_cum"], 16)
                pool.dma_start(cum_s[m][:], cu(1).broadcast_to([P, T])).then_inc(S["ld_cum"], 16)

        pool.wait_ge(S["x_out"], 16 * KB)
        pool.wait_ge(S["xl_s"], KB)
        load_kc("A", 0)
        pool.wait_ge(S["fchain"], 1)
        pool.memset(fones[:], 1.0).then_inc(S["pool1"], 1)
        pool.wait_ge(S["csum_d"], 3)
        pool.dma_start(c_scr[0, :, 0:T_P], csum[:, 0, 0:T_P]).then_inc(S["c_out"], 16)
        pool.dma_start(c_scr[1], csum[:, 1, :]).then_inc(S["c_out"], 16)
        pool.wait_ge(S["c_out"], 32)
        load_cum(0)
        pool.wait_ge(S["lfT_e"], 1)
        pool.dma_start(p_alogf.rearrange("o (t p) h -> (o p) t h", p=P), lf_tm[:, 0:8, :]).then_inc(S["lf_out"], 16)
        pool.dma_start(s_alogf[0], lf_tm[0:T_S, 8, :]).then_inc(S["lf_out"], 16)
        pool.wait_ge(S["x_out"], 16 * KB)
        pool.wait_ge(S["xl_s"], KB)
        pool.memset(v_tm[DH:P, 8, :], 0.0).then_inc(S["vpad"], 1)

        store_kv("k", "A", 0, k_tm, J1["KT2"])
        store_kv("v", "A", 0, v_tm, J1["VT2"])

        def body(U):
            u, loc = U.u, (U.u if U.kind == "A" else U.u - 4)
            if U.nxt:
                nk = U.next_kind
                un = (0 if nk != U.kind else loc + 1)
                hold(pool, "pj_f", U.j0, "hold_pool")
                load_kc(nk, un)
            hold(pool, "st_o", u * 16, "hold_pool")
            hold(pool, "norm_d", u + 1, "hold_pool")
            pool.dma_start(vc_raw, heads(c_av if U.kind == "A" else c_bv, 8)[loc]).then_inc(S["ld_vc"], 16)
            if U.nxt:
                store_kv("v", nk, un, v_tm, U.j0 + U.job["VT2"])
                store_kv("k", nk, un, k_tm, U.j0 + U.job["KT2"])
                if nk == "A":
                    hold(pool, "s_d", U.s0 + 18, "hold_pool")
                    load_cum(un)
            for g in range(2):
                hold(pool, "pj_d", U.j0 + U.job[f"G{g}2"], "hold_pool")
                pool.dma_start(gate_scr.rearrange("(u g) p t -> u g p t", g=2)[u][g], gate_st[g][:]
                               ).then_inc(S[f"st_g{g}"], 16)
                if g == 0 and U.kind == "A" and U.next_kind == "B":
                    pool.wait_ge(S["s_d"], U.s0 + 18)
                    pool.iota(dist_i, pattern=[[-1, T]], base=T - P, channel_multiplier=1).then_inc(S["dst"], 1)
                if g == 0 and U.nxt:
                    hold(pool, "pj_d", U.j0 + U.job["OT2"], "hold_pool")
                    pool.dma_start(o_scr[u], oT_st[:]).then_inc(S["st_o"], 16)

        units(pool, body)
        pool.wait_ge(S["pj_f"], J_PRO + 7 * J_UNIT + INDEX["B", False][0]["G12"])
        pool.wait_ge(S["st_o"], 16 * 7)
        pool.dma_start(o_all[:, 0:7, :], o_scr.rearrange("u p t -> p u t")).then_inc(S["ld_o"], 16)
        pool.wait_ge(S["av_f"], 72 + 36)
        pool.wait_ge(S["st_g0"], 16 * 8)
        pool.wait_ge(S["st_g1"], 16 * 8)
        pool.wait_ge(S["om_d"], 72 + 36)
        pool.wait_ge(S["pj_d"], J_PRO + 7 * J_UNIT + INDEX["B", False][0]["OT2"])
        for fb in range(KB):
            wait(pool, "gmul", 3 * fb)
            for g in range(2):
                pool.dma_start(gates[g][:], gate_scr[g * KB + fb]).then_inc(S["ld_g"], 16)
        pool.wait_ge(S["mg_f"], 3 * KB)
        pool.wait_ge(S["gmul"], 3 * KB)
        pool.wait_ge(S["m_l"], 3 * KB)
        pool.memset(ones4[:], 1.0 / D).then_inc(S["on4"], 1)
        for fb in range(KB):
            if fb >= 2:
                pool.wait_ge(S["x1_d"], 3 * (fb - 1))
            pool.dma_start(x_in[fb % 2][:], x_scr[fb]).then_inc(S[f"ld_xi{fb % 2}"], 16)
        pool.wait_ge(S["edgeT_e"], 2)
        for x, out in enumerate((p_conv, s_conv)):
            pool.dma_start(out[0].rearrange("r (b c) -> (r b) c", c=P), edge_rows[:, x, :]).then_inc(S["edge_o"], 16)
        yp = y_p.rearrange("o (t p) (i s c) -> i s (o p) t c", p=P, c=P, s=2)
        ys = y_s.rearrange("o p (i s c) -> i s (o p) c", c=P, s=2)
        with pool.Fori(0, 4) as i:
            for s in range(2):
                hold(pool, "yT_free", i * 6 + (3 * s + 6), "hold_pool")
                pool.dma_start(yp[i][s], y_tm[s][:, 0:8, :]).then_inc(S[f"y_o{s}"], 16)
                pool.dma_start(ys[i][s], y_tm[s][0:T_S, 8, :]).then_inc(S[f"y_o{s}"], 16)
        for name, value in (("lf_out", 32), ("st_v", 32 * 8), ("st_k", 32 * 8), ("edge_o", 32),
                            ("y_o0", 128), ("y_o1", 128)):
            pool.wait_ge(S[name], value)

    @block.tensor
    def _(pe):
        def mm(out, w, x, first, last, **kw):
            return pe.matmul(out, w, x, start=first, stop=last, **kw)

        def split_product(out, ws, xs, kblocks, tok, lo=0, hi=None):
            steps = [(k, ab) for k in kblocks for ab in PASSES]
            for i in range(lo, len(steps) if hi is None else hi):
                k, (a, b) = steps[i]
                r = mm(out, ws[a][:, k, :], xs[b][:, k, tok], i == 0, i == len(steps) - 1)
            return r

        pe.wait_ge(S["idt"], 2)
        pe.wait_ge(S["ld_xs"], 16)

        def square_sums(k):
            pe.wait_ge(S["sq_d"], k + 1)
            if k == 0:
                pe.wait_ge(S["cst"], 1)
            for c, (c0, n) in enumerate(CHUNKS):
                r = mm(three[c], all_ones[:], sq1[k % 2][:, c0:c0 + n], k == 0, k == KB - 1)
            r.then_inc(S["ms_f"], 1)

        for k in range(KB):
            if k % (KB // 2) == 0:
                pe.wait_ge(S[f"ld_x{k // (KB // 2)}"], 16)
            for part, (t0, t1, out) in enumerate(((0, 4, psT[:, 0:512]), (4, 8, psT[:, 512:1024]), (8, 9, psO[:, 0:T_S]))):
                wait(pe, "xT_e", 3 * (k - 1) + part + 1)
                for t in range(t0, t1):
                    if t < 8:
                        r = pe.transpose(out[:, P * (t - t0):P * (t - t0) + P], x_tm[:, t, P * k:P * k + P], ident[:])
                    else:
                        r = pe.transpose(out, x_tm[0:T_S, 8, P * k:P * k + P], ident[0:T_S, 0:T_S])
                r.then_inc(S["xT_f"], 1)
            if k >= 1:
                square_sums(k - 1)
        pe.wait_ge(S["ld_vec"], 16 * 8)
        pe.wait_ge(S["xT_e"], 3 * KB)
        for i in range(6):
            pe.transpose(psO[:, 44 * i:44 * i + 44], rows[0:44, i, :], ident[0:44, 0:44])
        for i in (6, 7):
            r = pe.transpose(psO[:, 264 + 8 * (i - 6):272 + 8 * (i - 6)], rows[0:KB, i, :], ident[0:KB, 0:KB])
        r.then_inc(S["vecT"], 1)
        square_sums(KB - 1)
        pe.wait_ge(S["ld_clog"], 16)
        for t in range(8):
            r = pe.transpose(psT[0:H_A, P * t:P * t + P], clog_tm[:, t, :], ident[:])
        r.then_inc(S["clT_f"], 1)

        def proj(bank, block_no, slot, c, lo, hi):
            if c == 0 and lo == 0:
                pe.wait_ge(S["wl_d"], block_no)
            c0, m = CHUNKS[c]
            return split_product(bank[:, 0:m], wsp[slot], xn, range(KB), slice(c0, c0 + m), lo, hi)

        def transposed(bank, src, tiles, tail_rows=T_S):
            for j, t in enumerate(tiles):
                n = T_S if t == 8 else P
                r = pe.transpose(bank[0:n, P * j:P * j + P], src[:, P * t:P * t + n], ident[:])
            return r


        def job(name, n, idx, base_of, U=None, lo=0, hi=None):
            bank = banks[(idx - 1) % 2]
            if lo == 0:
                wait(pe, "pj_d", n - 2)
                for x in range(2):
                    if idx - 2 == (J1 if U is None else U.job).get(f"KC{x}"):
                        pe.wait_ge(S["kcl_d"], (0 if U is None else U.u * 2 + 2) + x + 1)
            kind, c = name[:-1], int(name[-1])
            if kind in ("F", "Q", "K", "V", "G0", "G1"):
                if U is None:
                    no, slot = PROLOGUE_BLOCKS[kind]
                else:
                    no, slot = U.block(kind), SLOT[kind]
                r = proj(bank, no, slot, c, lo, hi)
                if hi is not None:
                    return
            elif kind == "SS":
                pe.wait_ge(S["pj_d"], base_of("QK"[c] + "2"))
                if U is None and c == 0:
                    pe.wait_ge(S["cst"], 5)
                for t in range(NT):
                    m = T_S if t == 8 else P
                    r = mm(bank[0:m, 2 * t:2 * t + 2], (sqq, sqk)[c][:, P * t:P * t + m], half_ones[:, 0:P:DH], True, True)
            elif kind in ("NQ", "NK"):
                if name == "NQ0":
                    pe.wait_ge(S["rt_d"], 1 if U is None else U.u + 2)
                pe.sem_inc(S["hold_pe"], 1)
                for j, t in enumerate(TGROUPS[c]):
                    m = T_S if t == 8 else P
                    for h in range(2):
                        src = root[0:m, t, "QK".index(kind[1]), h:h + 1].broadcast_to([m, DH])
                        r = mm(bank[DH * h:DH * h + DH, P * j:P * j + m], src, ident[0:m, 0:m], True, True)
            elif kind == "VT":
                pe.wait_ge(S["pj_d"], base_of("V2"))
                r = transposed(bank, zv, TGROUPS[c])
            elif kind == "KT":
                pe.wait_ge(S["norm_d"], 1 if U is None else U.u + 2)
                r = transposed(bank, zk, TGROUPS[c])
            elif kind == "KC":
                pe.wait_ge(S["ld_kc"], 16 if U is None else U.u * 16 + 32)
                for j in range(4):
                    r = pe.transpose(bank[:, P * j:P * j + P], kc_tm[:, 4 * c + j, :], ident[:])
            elif kind == "OT":
                if U.kind == "A":
                    pe.wait_ge(S["om_d"], U.g0 + 18)
                else:
                    pe.wait_ge(S["of_d"], U.u - 3)
                for j, t in enumerate(TGROUPS[c]):
                    r = pe.transpose(bank[:, P * j:P * j + P], o_tm[:, t, :], ident[:])
            r.then_inc(S["pj_f"], 1)

        for it in PROLOGUE_PLAN:
            if isinstance(it, str):
                if it == "F0":
                    pe.wait_ge(S["wl_d"], 2)
                    pe.wait_ge(S["vecD"], 1)
                    for k in range(KB):
                        pe.wait_ge(S["xl_s"], k + 1)
                        for n in range(6):
                            slot = PROLOGUE_BLOCKS["FQ"[n // 3]][1]
                            r = proj(first6[n], 1, slot, n % 3, 3 * k, 3 * k + 3)
                            if k == KB - 1:
                                r.then_inc(S["pj_f"], 1)
                elif J1[it] > 6:
                    job(it, J1[it], J1[it], lambda name: J1[name])
                if it == "V0":
                    pe.wait_ge(S["lf_d"], 1)
                    for t in range(NT):
                        n = T_S if t == 8 else P
                        r = pe.transpose(psO[0:n, 8 * t:8 * t + 8], logf[:, P * t:P * t + n], ident[0:H_A, 0:H_A])
                    r.then_inc(S["lfT_f"], 1)

        def body(U):
            u = U.u
            begun = None
            for it in U.plan:
                if it[0] in ("HALF", "J"):
                    idx = U.job[it[1]]
                    lo, hi = (12 if it[1] == begun else 0), (12 if it[0] == "HALF" else None)
                    job(it[1], U.j0 + idx, idx, lambda name: U.j0 + U.job[name], U, lo, hi)
                    begun = it[1] if it[0] == "HALF" else None
                elif it[0] == "S":
                    i, m = it[1:]
                    s = U.s[i, m]
                    wait(pe, "s_d", U.s0 + (s - 1))
                    if s == 1:
                        pe.wait_ge(S["spl_d"], u * 3 + 2)
                        if not isinstance(u, int) or u == 0:
                            pe.wait_ge(S["idr"], 2)
                    hr = slice(DH * m, DH * m + DH)
                    if i == 8:
                        q0, parts = T - P, [(kcs, 0, 512, 0), (kcs, 512, 512, 512), (ks, T_P, T_S, T_P)]
                        if m == 0:
                            pe.wait_ge(S["kcl_d"], u * 2 + 2)
                        diag, mcols = (T_P, T), slice(DH, P)
                    else:
                        q0, n = P * i, P * (i + 1)
                        parts = [(ks, c, min(512, n - c), c) for c in range(0, n, 512)]
                        diag, mcols = (P * i, P * i + P), slice(0, P)
                    for src, k0, n, at in parts:
                        masked = U.kind == "A" and at <= diag[0] < at + n
                        for x, (a, b) in enumerate(PASSES):
                            r = mm(psS[:, at:at + n], qs[a][hr, q0:q0 + P], src[b][hr, k0:k0 + n],
                                   x == 0, x == 2 and not masked)
                        if masked:
                            r = mm(psS[:, diag[0]:diag[1]], ident_r[:], mask_r[:, mcols], False, True)
                    r.then_inc(S["s_f"], 1)
                elif it[0] == "T":
                    i, m = it[1:]
                    g = U.g0 + U.grp[i, m]
                    if U.kind == "A":
                        pe.wait_ge(S["p_d"], U.s0 + U.s[i, m])
                    else:
                        pe.wait_ge(S["cb_d"], U.grp[i, m] + (U.u * 9 - 36))
                    wait(pe, "tl_d", g - 1)
                    src = sc[m]
                    if i == 8:
                        wait(pe, "o_d", g - 1)
                    for kb in range(8 if i == 8 else i + 1):
                        r = pe.transpose(psT[:, P * kb:P * kb + P], src[:, P * kb:P * kb + P], ident[:])
                    if i == 8:
                        r = pe.transpose(psO[0:T_S, 256:384], src[:, T_P:T], ident[:])
                    r.then_inc(S["t_f"], 1)
                elif it[0] == "AV":
                    i, m = it[1:]
                    g = U.g0 + U.grp[i, m]
                    if U.grp[i, m] == 1:
                        pe.wait_ge(S["spl_d"], u * 3 + 3)
                    pe.wait_ge(S["tl_d"], g)
                    wait(pe, "o_d", g - 1)
                    vc = slice(DH * m, DH * m + DH) if U.kind == "A" else slice(0, P)
                    w = vc.stop - vc.start
                    if i == 8:
                        if m == 0:
                            pe.wait_ge(S["vcl_d"], u + 1)
                        parts = [(vc_hl, kb, kb, P) for kb in range(8)] + [(v_hl, 8, 8, T_S)]
                    else:
                        parts = [(v_hl, kb, kb, P) for kb in range(i + 1)]
                    for x, (src, kb, tb, nk) in enumerate(parts):
                        last = x == len(parts) - 1
                        mm(psO[:, 0:2 * w], pt[0][0:nk, tb, :], src[0:nk, kb, :, vc], x == 0, False)
                        r = mm(psO[:, 0:w], pt[1][0:nk, tb, :], src[0:nk, kb, 0, vc], False, last)
                    r.then_inc(S["av_f"], 1)

        units(pe, body)

        def branch(s, x, tok, g, begin=False):
            out = (psS, psT)[g][:, 512 * x:512 * x + tok.stop - tok.start]
            for k in range(4):
                if begin:
                    pe.wait_ge(S["ol_d"], 4 * g + k + 1)
                r = split_product(out, wsp3[s], os_, range(4 * g, 4 * g + 4), tok, 3 * k, 3 * k + 3)
            return r

        def merge(i):
            for s in range(2):
                n3 = i * 2 + s
                pe.wait_ge(S["w3l"], n3 + 1)
                begin = isinstance(i, int) and s == 0
                if begin:
                    for c in range(2):
                        branch(s, c, slice(CHUNKS[c][0], sum(CHUNKS[c])), 0, True)
                for c, (c0, m) in enumerate(CHUNKS):
                    j = i * 6 + (3 * s + c)
                    if not isinstance(i, int) or j >= 2:
                        pe.wait_ge(S["gmul"], j - 1)
                    x = (3 * s + c) % 2
                    tok = slice(c0, c0 + m)
                    if not begin or c == 2:
                        branch(s, x, tok, 0)
                    branch(s, x, tok, 1, begin and c == 0).then_inc(S["mg_f"], 1)

        pe.wait_ge(S["o_d"], 108)
        merge(0)
        with pe.Fori(1, 4) as i:
            merge(i)

        pe.wait_ge(S["m_l"], 3 * KB)
        pe.wait_ge(S["ones_d"], 1)

        def sums4(fb):
            pe.wait_ge(S["sq4l"], fb + 1)
            for c, (c0, n) in enumerate(CHUNKS):
                for part in range(2):
                    r = mm(sums_out[c], ones_r[:], sq4s[fb % 2][part][:, c0:c0 + n],
                           fb == 0 and part == 0, fb == KB - 1 and part == 1)
            r.then_inc(S["ms4_f"], 1)

        for fb in range(KB):
            pe.wait_ge(S["w3l"], KB + fb + 1)
            for c, (c0, m) in enumerate(CHUNKS):
                j = 3 * fb + c
                wait(pe, "x1_d", j - 1)
                split_product(banks[j % 2][:, 0:m], wsp3[fb % 2], ms, range(KB), slice(c0, c0 + m)).then_inc(S["wo_f"], 1)
            if fb >= 1:
                sums4(fb - 1)

        pe.wait_ge(S["x1_d"], 3 * KB)
        blk, f0 = 2 * KB, 0
        for gi, ng in enumerate(GROUPS):
            pe.wait_ge(S["dn_free"], 24 * gi + 3)

            def up(i, h):
                pe.wait_ge(S["w3l"], i * 2 + (blk + h + 1))
                for c, (c0, m) in enumerate(CHUNKS):
                    x = 3 * h + c
                    pe.wait_ge(S["up_free"], i * 6 + (6 * f0 + x + 1))
                    split_product(ring_u[x][:, 0:m], wsp3[h], x2s, range(KB), slice(c0, c0 + m)
                                  ).then_inc(S["up_f"], 1)

            if gi == 0:
                pe.wait_ge(S["w3l"], blk + 1)
                pe.wait_ge(S["up_free"], 6)
                for k in range(KB):
                    pe.wait_ge(S["x2l"], k + 1)
                    for c, (c0, m) in enumerate(CHUNKS):
                        r = split_product(ring_u[c][:, 0:m], wsp3[0], x2s, range(KB), slice(c0, c0 + m), 3 * k, 3 * k + 3)
                        if k == KB - 1:
                            r.then_inc(S["up_f"], 1)
                    if k == 4:
                        sums4(KB - 1)
                pe.wait_ge(S["sqrt4"], 3)
                up(0, 1)
            with pe.Fori(1 if gi == 0 else 0, ng) as i:
                up(i, 0)
                up(i, 1)
            f0 += ng
            blk += 2 * ng
            final = gi == len(GROUPS) - 1
            pe.wait_ge(S["gl_free"], f0)
            pe.wait_ge(S["up_free"], 6 * f0 + 6)

            def down(i):
                for s in range(2):
                    pe.wait_ge(S["w3l"], i * 2 + (blk + s + 1))
                    for c, (c0, m) in enumerate(CHUNKS):
                        x = 3 * s + c
                        pe.wait_ge(S["dn_free"], i * 6 + (24 * gi + x + 1))
                        split_product(ring_d[c][:, 0:m], wsp3[s], gsp, range(ng), slice(c0, c0 + m), 0, 3 * ng - 3)
                    if isinstance(i, int) and s == 0:
                        pe.wait_ge(S["edge_d"], 2 * FB)
                        for x in range(2):
                            pe.transpose(psT[0:4 * FB, 512 * x:512 * x + P],
                                         edges[:, 2 * x:2 * x + 2, :].rearrange("p r b -> p (r b)"),
                                         ident[:]).then_inc(S["edgeT_f"], 1)
                    pe.wait_ge(S["gl_free"], f0 + 1)
                    for c, (c0, m) in enumerate(CHUNKS):
                        split_product(ring_d[c][:, 0:m], wsp3[s], gsp, range(ng), slice(c0, c0 + m), 3 * ng - 3
                                      ).then_inc(S["dn_f"], 1)
                    if final:
                        if s == 0:
                            pe.wait_ge(S["edgeT_e"], 2)
                        for part, out in enumerate((psT[:, 0:512], psT[:, 512:1024], psS[:, 0:512])):
                            x = 3 * s + part
                            pe.wait_ge(S["yT_free"], i * 6 + (x + 1))
                            if part == 0:
                                pe.wait_ge(S["dn_free"], i * 6 + (24 * gi + 3 * s + 6))
                            for j, t in enumerate(TGROUPS[part]):
                                n = T_S if t == 8 else P
                                r = pe.transpose(out[0:n, P * j:P * j + P], y_blk[s][:, P * t:P * t + n], ident[:])
                            r.then_inc(S["yT_f"], 1)

            if final:
                down(0)
            with pe.Fori(1 if final else 0, 4) as i:
                down(i)
            blk += 8

    @block.scalar
    def _(act):
        def copy(out, in_, **kw):
            return act.activation(out, in_, ACT.Copy, **kw)

        act.wait_ge(S["idt"], 2)
        copy(ident_r[:], ident[:]).then_inc(S["idr"], 1)
        act.wait_ge(S["msk"], 2)
        copy(mask_r[:], maskf[:]).then_inc(S["idr"], 1)

        def w_high(slot, number, sem_name=None, value=None):
            act.wait_ge(S["wraw_s"], number * 16)
            if sem_name:
                act.wait_ge(S[sem_name], value)
            copy(wsp[slot][0][:], wraw[:]).then_inc(S["wh_d"], 1)

        for k in range(KB):
            for part, (a, b, src) in enumerate(((0, 512, psT[:, 0:512]), (512, 1024, psT[:, 512:1024]), (1024, T, psO[:, 0:T_S]))):
                act.wait_ge(S["xT_f"], 3 * k + part + 1)
                copy(xT[:, k, a:b], src).then_inc(S["xT_e"], 1)
            if k == 3:
                w_high(1, 1)
            elif k == 7:
                w_high(0, 2)
        act.wait_ge(S["vecT"], 1)
        copy(vecs[:, 0:280], psO[:, 0:280]).then_inc(S["vecD"], 1)
        act.wait_ge(S["ms_f"], KB)
        act.wait_ge(S["cst"], 2)
        for c, (c0, n) in enumerate(CHUNKS):
            act.activation(rstd1[:, c0:c0 + n], three[c], ACT.Sqrt, bias=eps_t).then_inc(S["sqrt1"], 1)

        for k in range(KB):
            act.wait_ge(S["xh_d"], k + 1)
            copy(xn[0][:, k, :], sq1[k % 2][:]).then_inc(S["xh_s"], 1)
            if k == 3:
                act.wait_ge(S["clT_f"], 1)
                copy(clog[:], psT[0:H_A, 0:PAST]).then_inc(S["clT_e"], 1)

        def evacuate(name, n, idx, base_of, U=None):
            bank = first6[idx - 1] if U is None and idx <= 6 else banks[(idx - 1) % 2]
            kind, c = name[:-1], int(name[-1])
            u = 0 if U is None else U.u + 1
            act.wait_ge(S["pj_f"], n)
            if kind in ("F", "Q", "K", "V", "G0", "G1"):
                c0, m = CHUNKS[c]
                src, tok = bank[:, 0:m], slice(c0, c0 + m)
            if kind == "F":
                if c == 0:
                    act.wait_ge(S["small_d"], 1)
                r = act.activation(fz[:, tok], bank[0:H_A, 0:m], ACT.Identity, bias=bf_t)
            elif kind in ("Q", "K"):
                z, q = (zq, sqq) if kind == "Q" else (zk, sqk)
                if c == 0:
                    if U is None:
                        act.wait_ge(S["x_out"], 16 * KB)
                        act.wait_ge(S["xl_s"], KB)
                    else:
                        act.wait_ge(S["spl_d"], U.u * 3 + 3)
                        if kind == "Q":
                            wait(act, "st_g1", U.u * 16)
                        else:
                            act.wait_ge(S["vcl_d"], U.u + 1)
                copy(z[:, tok], src)
                r = act.activation(q[:, tok], src, ACT.Square)
            elif kind == "V":
                if c == 0 and U is not None:
                    wait(act, "st_g0", U.u * 16)
                r = copy(zv[:, tok], src)
            elif kind == "SS":
                r = copy(meansq[:, 0:8, c, :], bank[:, 0:16].rearrange("p (t h) -> p t h", h=2))
                r = copy(meansq[0:T_S, 8, c, :], bank[0:T_S, 16:18])
            elif kind in ("NQ", "NK"):
                t0, m = TGROUPS[c][0] * P, (3 * P if c < 2 else 2 * P + T_S)
                r = copy((sqq if kind == "NQ" else sqk)[:, t0:t0 + m], bank[:, 0:m])
            elif kind in ("VT", "KT"):
                dst = v_tm if kind == "VT" else k_tm
                if c == 0 and U is not None:
                    if kind == "VT":
                        act.wait_ge(S["st_v"], U.u * 32 + 32)
                        act.wait_ge(S["spl_d"], U.u * 3 + 3)
                    else:
                        act.wait_ge(S["st_k"], U.u * 32 + 32)
                whole = 3 if c < 2 else 2
                r = copy(dst[:, 3 * c:3 * c + whole, :], bank[:, 0:whole * P].rearrange("p (t c) -> p t c", c=P))
                if c == 2:
                    r = copy(dst[0:T_S, 8, :], bank[0:T_S, 2 * P:3 * P])
            elif kind == "KC":
                if U is not None:
                    act.wait_ge(S["s_f"], U.s0 + U.s[8, 1])
                r = copy(kcs[0][:, 512 * c:512 * c + 512], bank[:])
            elif kind in ("G0", "G1"):
                g = int(kind[1])
                if c == 0 and not U.nxt:
                    act.wait_ge(S[f"st_g{g}"], U.u * 16)
                if c == 0 and U.nxt and g == 1:
                    act.wait_ge(S["norm_d"], U.u + 2)
                r = act.activation(gate_st[g][:, tok], src, ACT.Tanh, scale=0.5)
            elif kind == "OT":
                if c == 0:
                    act.wait_ge(S["vcl_d"], U.u + 1)
                kw = {} if U.kind == "A" else {"scale": sub_g}
                whole = (3 if c < 2 else 2) * P
                dst = oT_st if U.nxt else o_all[:, UNITS - 1, :]
                r = copy(dst[:, 3 * P * c:3 * P * c + whole], bank[:, 0:whole], **kw)
                if c == 2:
                    r = copy(dst[:, T_P:T], bank[:, 2 * P + DH:3 * P], **kw)
            r.then_inc(S["pj_d"], 1)

        def norm_roots(U=None):
            act.wait_ge(S["pj_d"], J1["SS1"] if U is None else U.j0 + U.job["SS1"])
            if U is None:
                act.wait_ge(S["ms_pad"], 1)
            else:
                act.wait_ge(S["pj_f"], U.j0)
            act.activation(root[:], meansq[:], ACT.Sqrt, bias=eps_t).then_inc(S["sq_rt"], 1)

        def split_qkv(U=None, parts=(0, 1, 2)):
            if U is None:
                if 0 in parts:
                    act.wait_ge(S["norm_d"], 1)
                    act.wait_ge(S["lf_out"], 32)
                    act.wait_ge(S["c_out"], 32)
                else:
                    act.wait_ge(S["pj_d"], J1["VT2"])
                    act.wait_ge(S["vpad"], 1)
            else:
                act.wait_ge(S["norm_d"], U.u + 2)
                act.wait_ge(S["s_f"], U.s0 + 18)
                act.wait_ge(S["av_f"], U.g0 + (18 if U.kind == "A" else 9))
                act.wait_ge(S["pj_d"], U.j0 + U.job["VT2"])
            for part in parts:
                high, whole = ((qs[0][:], zq[:]), (ks[0][:], zk[:]), (v_hl[:, :, 0, :], v_tm[:]))[part]
                copy(high, whole).then_inc(S["sph_d"], 1)

        for it in PROLOGUE_PLAN:
            if isinstance(it, str):
                evacuate(it, J1[it], J1[it], lambda name: J1[name])
                if it == "V0":
                    act.wait_ge(S["lfT_f"], 1)
                    copy(lf_tm[:, 0:8, :], psO[:, 0:64].rearrange("p (t h) -> p t h", h=8))
                    copy(lf_tm[0:T_S, 8, :], psO[0:T_S, 64:72]).then_inc(S["lfT_e"], 1)
            elif it[0] == "FORGET":
                act.wait_ge(S["lam_v"], 3)
                act.activation(lamt[:, 130:132], lamt[:, 128:130], ACT.Exp).then_inc(S["lam_a"], 1)
                act.wait_ge(S["pj_d"], J1["F2"])
                act.activation(fa[:], fz[:], ACT.Abs).then_inc(S["fz_e"], 1)
                act.wait_ge(S["fz_e"], 1)
                act.activation(fa[:], fa[:], ACT.Exp, scale=-1.0).then_inc(S["fz_e"], 1)
                act.wait_ge(S["fz_e"], 2)
                act.activation(fa[:], fa[:], ACT.Ln, bias=one_t[0:H_A]).then_inc(S["fz_e"], 1)
            elif it[0] == "W" and it[1] in ("K", "V"):
                no, slot = PROLOGUE_BLOCKS[it[1]]
                w_high(slot, no, "pj_f", J1["F2" if it[1] == "K" else "Q2"])
            elif it[0] == "WFIRST":
                w_high(0, 5, "pj_f", J1["V2"])
            elif it[0] == "NORM":
                norm_roots()
            elif it[0] == "SPLIT":
                split_qkv(parts=it[1:])

        def body(U):
            u = U.u
            for it in U.plan:
                if it[0] == "J":
                    idx = U.job[it[1]]
                    evacuate(it[1], U.j0 + idx, idx, lambda name: U.j0 + U.job[name], U)
                elif it[0] == "VC":
                    act.wait_ge(S["ld_vc"], u * 16 + 16)
                    wait(act, "av_f", U.g0)
                    copy(vc_hl[:, :, 0, :], vc_raw).then_inc(S["vch_d"], 1)
                elif it[0] == "S":
                    i, m = it[1:]
                    n = keys_of(i)
                    act.wait_ge(S["s_d"], U.s0 + U.s[i, m])
                    act.activation(sc[m][:, 0:n], sc[m][:, 0:n], ACT.Exp, bias=smin[:, m:m + 1], scale=-1.0,
                                   accum_out=den[:, m:m + 1]).then_inc(S["p_d"], 1)
                elif it[0] == "T":
                    i, m = it[1:]
                    g = U.g0 + U.grp[i, m]
                    act.wait_ge(S["t_f"], g)
                    wait(act, "av_f", g - 1)
                    nb = 8 if i == 8 else i + 1
                    r = copy(pt[0][:, 0:nb, :], psT[:, 0:P * nb].rearrange("p (t c) -> p t c", c=P))
                    if i == 8:
                        r = copy(pt[0][0:T_S, 8, :], psO[0:T_S, 256:384])
                    r.then_inc(S["th_d"], 1)
                elif it[0] == "AV":
                    i, m = it[1:]
                    g = U.g0 + U.grp[i, m]
                    act.wait_ge(S["o_d"], g)
                    if U.kind == "A":
                        act.wait_ge(S["rd_d"], g)
                        part = o_tm[:, i, DH * m:DH * m + DH]
                        copy(part, part, scale=rden[:, m:m + 1]).then_inc(S["om_d"], 1)
                    else:
                        act.activation(junk[:], o_tm[:, i, :], ACT.Square, scale=inv0[:, i:i + 1],
                                       accum_out=sumsq[:, i:i + 1]).then_inc(S["om_d"], 1)
                elif it[0] == "H":
                    name = it[1]
                    before = {"K": U.j0, "V": U.j0 + U.job.get("Q2", 0), "G0": U.j0 + U.job.get("V2", 0),
                              "G1": U.j0 + U.job.get("K2", 0), "FIRST": U.j0 + U.job["G02"]}[name]
                    w_high(SLOT[name], U.block(name), "pj_f", before)
                elif it[0] == "ROOT":
                    norm_roots(U)
                elif it[0] == "SPLIT":
                    split_qkv(U)
                    if U.kind == "A" and U.next_kind == "B":
                        act.wait_ge(S["dst"], 1)
                        act.activation(dist, dist_i, ACT.Abs).then_inc(S["dst_a"], 1)
                elif it[0] == "OFIN" and U.kind == "B":
                    act.wait_ge(S["om_d"], U.g0 + 9)
                    act.activation(rsub, sumsq, ACT.Sqrt, bias=eps_t, scale=1.0 / P).then_inc(S["rs_d"], 1)

        units(act, body)

        def w3_high(s, loaded, sem_name, value):
            act.wait_ge(S[f"w3_s{s}"], loaded)
            wait(act, sem_name, value)
            copy(wsp3[s][0][:], wraw3[s][:]).then_inc(S["w3h"], 1)

        last = J_PRO + 7 * J_UNIT
        w3_high(0, 32, "pj_f", last + INDEX["B", False][0]["G12"])
        w3_high(1, 32, "pj_f", last)
        act.wait_ge(S["st_o"], 16 * 7)
        act.wait_ge(S["st_v"], 256)
        act.wait_ge(S["st_k"], 256)
        act.wait_ge(S["av_f"], 108)
        act.wait_ge(S["o_d"], 108)
        act.wait_ge(S["of_d"], 4)
        for k in range(UNITS):
            if k < UNITS - 1:
                act.wait_ge(S["ld_o"], 16)
            else:
                act.wait_ge(S["pj_d"], last + INDEX["B", False][0]["OT2"])
            copy(os_[0][:, k, :], o_all[:, k, :]).then_inc(S["oh_d"], 1)

        def merge(i):
            for s in range(2):
                for c, (c0, m) in enumerate(CHUNKS):
                    j, x = i * 6 + (3 * s + c), (3 * s + c) % 2
                    act.wait_ge(S["mg_d"], j + 1)
                    if isinstance(i, int) and j == 0:
                        act.wait_ge(S["ol_d"], UNITS)
                    copy(ms[0][:, i * 2 + s, c0:c0 + m], mt[x][0][:, 0:m], scale=0.5).then_inc(S["m_h"], 1)
                w3_high(s, (i * 32 + 64) if (isinstance(i, int) and i < 3) or not isinstance(i, int) else 144,
                        "mg_f", i * 6 + (3 * s + 3))

        merge(0)
        with act.Fori(1, 3) as i:
            merge(i)
        merge(3)

        act.wait_ge(S["on4"], 1)
        copy(ones_r[:], ones4[:]).then_inc(S["ones_d"], 1)

        def square4(fb):
            act.wait_ge(S["x1_d"], 3 * fb + 3)
            wait(act, "ms4_f", fb - 1)
            act.activation(sq4[fb % 2][:], x1[:, fb, :], ACT.Square).then_inc(S["sq4_d"], 1)
            act.wait_ge(S["sq4_d"], fb + 1)
            copy(sq4s[fb % 2][0][:], sq4[fb % 2][:]).then_inc(S["sq4h"], 1)

        for fb in range(KB):
            if fb < KB - 1:
                square4(fb)
            w3_high(fb % 2, 128 + 16 * (fb // 2 + 2), "wo_f", 3 * fb + 3)
        act.wait_ge(S["x1_d"], 3 * KB)
        for k in range(KB):
            copy(x2s[0][:, k, :], x1[:, k, :], scale=gain_ffn[:, k:k + 1]).then_inc(S["x2h"], 1)
            if k == 1:
                square4(KB - 1)
        act.wait_ge(S["ms4_f"], KB)
        for c, (c0, n) in enumerate(CHUNKS):
            act.activation(rstd4[:, c0:c0 + n], sums_out[c], ACT.Sqrt, bias=eps_t).then_inc(S["sqrt4"], 1)

        act.sem_inc(S["yT_free"], 3)
        act.wait_ge(S["pads"], 4)
        pair, f0 = 8, 0
        state = cstate.rearrange("p (r b) -> p b r", r=2)
        for gi, ng in enumerate(GROUPS):
            if gi:
                act.wait_ge(S["dn_f"], 24 * gi)
            with act.Fori(0, ng) as i:
                done = i * 6 + 6 * f0
                for h in range(2):
                    act.wait_ge(S["u_free"], i * 2 + (2 * f0 + h + 1))
                    copy(ub[h][:, T_P + 2:T_P + 4], state[:, i + (f0 + FB * h), :]).then_inc(S["state_d"], 1)
                    act.wait_ge(S["state_d"], i * 2 + (2 * f0 + h + 1))
                    act.wait_ge(S["up_free"], i * 6 + (6 * f0 + 3 * h + 9))
                    act.wait_ge(S["gl_free"], i + (f0 + 1))
                    b = i + (f0 + FB * h)
                    act.activation(ct[h][:], ub[h][:, 2:TU], ACT.Identity, scale=taps[2][:, bass.ds(b, 1)],
                                   bias=cbias[:, bass.ds(b, 1)]).then_inc(S["ct_a"], 1)
                    if h == 1:
                        act.wait_ge(S["u_free"], i * 2 + (2 * f0 + 3))
                        act.activation(ct[0][:], ct[0][:], ACT.Silu).then_inc(S["silu_d"], 1)
                    act.wait_ge(S[f"w3_s{h}"], i * 16 + (64 + 16 * (pair + 2)))
                    copy(wsp3[h][0][:], wraw3[h][:]).then_inc(S["w3h"], 1)
                act.wait_ge(S["gm_d"], i + (f0 + 1))
                copy(gsp[0][:, i, 0:T_P], ct[1][:, 0:T_P])
                copy(gsp[0][:, i, T_P:T], ct[1][:, T_P + 2:TU - 2]).then_inc(S["gh_d"], 1)
            pair += ng
            f0 += ng
            final = gi == len(GROUPS) - 1
            if final:
                for x in range(2):
                    act.wait_ge(S["edgeT_f"], x + 1)
                    copy(edge_rows[:, x, :], psT[0:4 * FB, 512 * x:512 * x + P]).then_inc(S["edgeT_e"], 1)

            def down(i):
                for s in range(2):
                    if not (final and isinstance(i, int) and i == 3):
                        act.wait_ge(S[f"w3_s{s}"], i * 16 + (64 + 16 * (pair + 2)))
                        act.wait_ge(S["dn_f"], i * 6 + (24 * gi + 3 * s + 3))
                        copy(wsp3[s][0][:], wraw3[s][:]).then_inc(S["w3h"], 1)
                    if final:
                        wait(act, f"y_o{s}", i * 32)
                        for part in range(3):
                            act.wait_ge(S["yT_f"], i * 6 + (3 * s + part + 1))
                            bank = (psT[:, 0:512], psT[:, 512:1024], psS[:, 0:512])[part]
                            whole = 3 if part < 2 else 2
                            r = copy(y_tm[s][:, 3 * part:3 * part + whole, :],
                                     bank[:, 0:whole * P].rearrange("p (t c) -> p t c", c=P))
                            if part == 2:
                                r = copy(y_tm[s][0:T_S, 8, :], bank[0:T_S, 2 * P:3 * P])
                            r.then_inc(S["yT_free"], 1)

            if final:
                down(0)
                with act.Fori(1, 3) as i:
                    down(i)
                down(3)
            else:
                with act.Fori(0, 4) as i:
                    down(i)
            pair += 4

    @block.vector
    def _(dve):
        chain = [0]

        def link(ins, name="fchain"):
            chain[0] += 1
            ins.then_inc(S["dchain"], 1)
            dve.wait_ge(S["dchain"], chain[0])

        def high_of(t):
            return t.bitcast(F32)

        def rest(out, in_, high):
            return dve.tensor_tensor(out, in_, high_of(high), ALU.subtract)

        dve.memset(one_t, 1.0)
        dve.memset(meansq[:, 8, :, :], 1.0).then_inc(S["ms_pad"], 1)

        def w_low(slot, number):
            dve.wait_ge(S["wh_d"], number)
            rest(wsp[slot][1][:], wraw[:], wsp[slot][0][:]).then_inc(S["wl_d"], 1)

        for k in range(KB):
            dve.wait_ge(S["xT_e"], 3 * k + 3)
            wait(dve, "ms_f", k - 1)
            dve.tensor_tensor(sq1[k % 2][:], xT[:, k, :], xT[:, k, :], ALU.mult).then_inc(S["sq_d"], 1)
            if k == 4:
                w_low(1, 1)
        w_low(0, 2)
        dve.wait_ge(S["ld_small"], 16 * 14)
        dve.tensor_scalar(gq_a, gq_a, -DH ** -0.5, None, ALU.mult)
        dve.tensor_scalar(gq_b, gq_b, -DH ** -0.5, None, ALU.mult)
        dve.tensor_scalar(sub_g, sub_g, 1.0 - LAMBDA_INIT, None, ALU.mult).then_inc(S["small_d"], 1)
        dve.tensor_tensor(lamt[:, 0:DH], lamv[:, 0, :], lamv[:, 1, :], ALU.mult).then_inc(S["lam_v"], 1)
        dve.tensor_tensor(lamt[:, DH:2 * DH], lamv[:, 2, :], lamv[:, 3, :], ALU.mult).then_inc(S["lam_v"], 1)
        dve.wait_ge(S["lam_v"], 2)
        dve.tensor_reduce(out=lamt[:, 128:130], in_=lamt[:, 0:128].rearrange("p (a d) -> p a d", a=2),
                          axis=AX, op=ALU.add).then_inc(S["lam_v"], 1)
        dve.wait_ge(S["sqrt1"], 3)
        link(dve.reciprocal(rstd1[:], rstd1[:]))

        def x_scaled(k):
            wait(dve, "xh_s", k - 1)
            dve.scalar_tensor_tensor(sq1[k % 2][:], xT[:, k, :], gain_attn[:, k:k + 1], rstd1[:],
                                     ALU.mult, ALU.mult).then_inc(S["xh_d"], 1)

        def x_low(k):
            dve.wait_ge(S["xh_s"], k + 1)
            rest(xn[1][:, k, :], sq1[k % 2][:], xn[0][:, k, :]).then_inc(S["xl_s"], 1)

        dve.wait_ge(S["ms_f"], KB)
        dve.wait_ge(S["vecD"], 1)
        x_scaled(0)
        for k in range(1, KB):
            if k >= 2:
                dve.wait_ge(S["xl_s"], k - 1)
            x_scaled(k)
            x_low(k - 1)
        x_low(KB - 1)

        def invert_roots(U=None):
            dve.wait_ge(S["sq_rt"], 1 if U is None else U.u + 2)
            dve.reciprocal(root[:], root[:]).then_inc(S["rt_d"], 1)

        def normalize(U=None):
            kind = "A" if U is None else U.next_kind
            for name, z, q, g in (("NQ2", zq, sqq, gq_a if kind == "A" else gq_b),
                                  ("NK2", zk, sqk, gk_a if kind == "A" else gk_b)):
                dve.wait_ge(S["pj_d"], J1[name] if U is None else U.j0 + U.job[name])
                r = dve.scalar_tensor_tensor(z[:], z[:], g, q[:], ALU.mult, ALU.mult)
            r.then_inc(S["norm_d"], 1)

        def split_qkv(U=None, parts=(0, 1, 2)):
            n = 0 if U is None else U.u * 3 + 3
            for part in parts:
                low, whole, high = ((qs[1][:], zq[:], qs[0][:]), (ks[1][:], zk[:], ks[0][:]),
                                    (v_hl[:, :, 1, :], v_tm[:], v_hl[:, :, 0, :]))[part]
                dve.wait_ge(S["sph_d"], n + part + 1)
                rest(low, whole, high).then_inc(S["spl_d"], 1)

        def cached_k_low(n, bank, c):
            dve.wait_ge(S["pj_d"], n)
            rest(kcs[1][:, 512 * c:512 * c + 512], bank[:], kcs[0][:, 512 * c:512 * c + 512]).then_inc(S["kcl_d"], 1)

        LINKS = 12

        for it in PROLOGUE_PLAN:
            if isinstance(it, str):
                if it[:2] == "KC":
                    cached_k_low(J1[it], banks[(J1[it] - 1) % 2], int(it[2]))
            elif it[0] == "FORGET":
                dve.wait_ge(S["lam_a"], 1)
                link(dve.tensor_tensor(neg_lam, lamt[:, 131:132], lamt[:, 130:131], ALU.subtract))
                link(dve.tensor_scalar(neg_lam, neg_lam, -LAMBDA_INIT, None, ALU.add))
                dve.wait_ge(S["fz_e"], 3)
                dve.tensor_scalar(fz[:], fz[:], 0.0, None, ALU.min).then_inc(S["fchain"], 1)
                dve.wait_ge(S["fchain"], 1)
                dve.tensor_tensor(logf[:], fz[:], fa[:], ALU.subtract).then_inc(S["lf_d"], 1)
                dve.wait_ge(S["lf_d"], 1)
                dve.wait_ge(S["pool1"], 1)
                dve.wait_ge(S["clT_e"], 1)
                dve.tensor_tensor_scan(csum[:, 0, 0:T_P], fones[:, 0:T_P], logf[:, 0:T_P], 0.0,
                                       ALU.mult, ALU.add).then_inc(S["csum_d"], 1)
                dve.tensor_tensor_scan(csum[:, 1, 0:PAST], fones[:, 0:PAST], clog[:], 0.0,
                                       ALU.mult, ALU.add).then_inc(S["csum_d"], 1)
                dve.wait_ge(S["csum_d"], 2)
                dve.tensor_tensor_scan(csum[:, 1, PAST:T], fones[:, PAST:T], logf[:, T_P:T],
                                       csum[:, 1, PAST - 1:PAST], ALU.mult, ALU.add).then_inc(S["csum_d"], 1)
            elif it[0] == "W" and it[1] in ("K", "V"):
                no, slot = PROLOGUE_BLOCKS[it[1]]
                w_low(slot, no)
            elif it[0] == "WFIRST":
                w_low(0, 5)
            elif it[0] == "NORM":
                invert_roots()
            elif it[0] == "SCALE":
                normalize()
            elif it[0] == "SPLIT":
                split_qkv(parts=it[1:])

        def body(U):
            u = U.u
            links = 0 if U.kind == "A" else u * LINKS - 4 * LINKS
            n_link = 0
            for it in U.plan:
                if it[0] == "J" and it[1][:2] == "KC":
                    idx = U.job[it[1]]
                    cached_k_low(U.j0 + idx, banks[(idx - 1) % 2], int(it[1][2]))
                elif it[0] == "GS" and U.kind == "B":
                    dve.wait_ge(S["dst_m"], 1)
                    dve.tensor_scalar(dist, dist, 0.25, None, ALU.mult).then_inc(S["dch"], 1)
                    n_link += 1
                    dve.wait_ge(S["dch"], links + n_link)
                elif it[0] == "VC":
                    dve.wait_ge(S["vch_d"], u + 1)
                    rest(vc_hl[:, :, 1, :], vc_raw, vc_hl[:, :, 0, :]).then_inc(S["vcl_d"], 1)
                elif it[0] == "S":
                    i, m = it[1:]
                    n = keys_of(i)
                    if U.kind == "A":
                        if (i, m) == (7, 0):
                            dve.wait_ge(S["ld_cum"], u * 64 + 64)
                        term = (cum_s if i == 8 else cum_p)[m][:, 0:n]
                    else:
                        term = dist[:, 0:T] if i == 8 else dist[:, T - n:T]
                    hold(dve, "s_f", U.s0 + U.s[i, m], "hold_dve")
                    dve.tensor_tensor_reduce(out=sc[m][:, 0:n], in0=psS[:, 0:n], in1=term, scale=1.0, scalar=3e38,
                                             op0=ALU.add, op1=ALU.min, accum_out=smin[:, m:m + 1]
                                             ).then_inc(S["s_d"], 1)
                elif it[0] == "C":
                    i, n = it[1], keys_of(it[1])
                    c = U.grp[i, 0]
                    dve.wait_ge(S["p_d"], U.s0 + U.s[i, 1])
                    dve.reciprocal(inv0[:, i:i + 1], den[:, 0:1])
                    dve.reciprocal(rden[:, 1:2], den[:, 1:2]).then_inc(S["dch"], 1)
                    n_link += 1
                    dve.wait_ge(S["dch"], links + n_link)
                    dve.scalar_tensor_tensor(rden[:, 0:1], rden[:, 1:2], neg_lam, den[:, 0:1],
                                             ALU.mult, ALU.mult).then_inc(S["rd_d"], 1)
                    dve.wait_ge(S["rd_d"], 72 + c + (u * 9 - 36))
                    dve.scalar_tensor_tensor(sc[0][:, 0:n], sc[1][:, 0:n], rden[:, 0:1], sc[0][:, 0:n],
                                             ALU.mult, ALU.add).then_inc(S["cb_d"], 1)
                elif it[0] == "T":
                    i, m = it[1:]
                    g = U.g0 + U.grp[i, m]
                    dve.wait_ge(S["th_d"], g)
                    nb = 8 if i == 8 else i + 1
                    r = rest(pt[1][:, 0:nb, :], psT[:, 0:P * nb].rearrange("p (t c) -> p t c", c=P), pt[0][:, 0:nb, :])
                    if i == 8:
                        r = rest(pt[1][0:T_S, 8, :], psO[0:T_S, 256:384], pt[0][0:T_S, 8, :])
                    r.then_inc(S["tl_d"], 1)
                    if U.kind == "A":
                        dve.reciprocal(rden[:, m:m + 1], den[:, m:m + 1]).then_inc(S["rd_d"], 1)
                elif it[0] == "AV":
                    i, m = it[1:]
                    g = U.g0 + U.grp[i, m]
                    dve.wait_ge(S["av_f"], g)
                    if U.grp[i, m] == 1 and (not isinstance(u, int) or u > 0):
                        dve.wait_ge(S["pj_f"], U.j0)
                    w = DH if U.kind == "A" else P
                    dve.tensor_reduce(out=o_tm[:, i, w * m:w * m + w], in_=psO[:, 0:2 * w].rearrange("p (a d) -> p d a", a=2),
                                      axis=AX, op=ALU.add).then_inc(S["o_d"], 1)
                elif it[0] == "L":
                    w_low(SLOT[it[1]], U.block(it[1]))
                elif it[0] == "RD":
                    invert_roots(U)
                elif it[0] == "SCALE":
                    normalize(U)
                elif it[0] == "SPLIT":
                    split_qkv(U)
                    if U.kind == "A" and U.next_kind == "B":
                        dve.wait_ge(S["dst_a"], 1)
                        dve.memset(dist[0:DH, T - DH:T], BIG).then_inc(S["dst_m"], 1)
                elif it[0] == "OFIN" and U.kind == "B":
                    dve.wait_ge(S["rs_d"], u - 3)
                    dve.reciprocal(rsub, rsub).then_inc(S["dch"], 1)
                    dve.wait_ge(S["dch"], links + n_link + 1)
                    dve.tensor_tensor(rsub, rsub, inv0[:], ALU.mult).then_inc(S["dch"], 1)
                    n_link += 2
                    dve.wait_ge(S["dch"], links + n_link)
                    dve.tensor_tensor(o_tm[:], o_tm[:], rsub.rearrange("p (t a) -> p t a", a=1).broadcast_to([P, NT, P]),
                                      ALU.mult).then_inc(S["of_d"], 1)
            assert not U.nxt or n_link == (0 if U.kind == "A" else LINKS)

        units(dve, body)

        def w3_low(s, number):
            dve.wait_ge(S["w3h"], number)
            rest(wsp3[s][1][:], wraw3[s][:], wsp3[s][0][:]).then_inc(S["w3l"], 1)

        w3_low(0, 1)
        w3_low(1, 2)
        for k in range(UNITS):
            dve.wait_ge(S["oh_d"], k + 1)
            rest(os_[1][:, k, :], o_all[:, k, :], os_[0][:, k, :]).then_inc(S["ol_d"], 1)

        def merge(i):
            for s in range(2):
                for c, (c0, m) in enumerate(CHUNKS):
                    j, x = i * 6 + (3 * s + c), (3 * s + c) % 2
                    if c == 0:
                        dve.wait_ge(S["ld_g"], i * 64 + (32 * s + 32))
                    dve.wait_ge(S["mg_f"], j + 1)
                    for g, bank in ((0, psS), (1, psT)):
                        r = dve.scalar_tensor_tensor(mt[x][g][:, 0:m], gates[g][:, c0:c0 + m], 1.0,
                                                     bank[:, 512 * x:512 * x + m], ALU.add, ALU.mult)
                    r.then_inc(S["gmul"], 1)
                    dve.wait_ge(S["gmul"], j + 1)
                    dve.tensor_tensor(mt[x][0][:, 0:m], mt[x][0][:, 0:m], mt[x][1][:, 0:m], ALU.add).then_inc(S["mg_d"], 1)
                    dve.wait_ge(S["m_h"], j + 1)
                    dve.scalar_tensor_tensor(ms[1][:, i * 2 + s, c0:c0 + m], mt[x][0][:, 0:m], 0.5,
                                             high_of(ms[0][:, i * 2 + s, c0:c0 + m]), ALU.mult, ALU.subtract
                                             ).then_inc(S["m_l"], 1)
                w3_low(s, i * 2 + (s + 3))

        with dve.Fori(0, 4) as i:
            merge(i)

        def square_low(fb):
            dve.wait_ge(S["sq4h"], fb + 1)
            rest(sq4s[fb % 2][1][:], sq4[fb % 2][:], sq4s[fb % 2][0][:]).then_inc(S["sq4l"], 1)

        for fb in range(KB):
            for c, (c0, m) in enumerate(CHUNKS):
                j = 3 * fb + c
                dve.wait_ge(S["wo_f"], j + 1)
                if c == 0:
                    dve.wait_ge(S[f"ld_xi{fb % 2}"], 16 * (fb // 2 + 1))
                dve.tensor_tensor(x1[:, fb, c0:c0 + m], banks[j % 2][:, 0:m], x_in[fb % 2][:, c0:c0 + m],
                                  ALU.add).then_inc(S["x1_d"], 1)
            if fb < KB - 1:
                square_low(fb)
            w3_low(fb % 2, KB + 2 + fb + 1)
        dve.sem_inc(S["up_free"], 6)
        dve.sem_inc(S["dn_free"], 3)
        dve.wait_ge(S["x1_d"], 3 * KB)
        for k in range(KB):
            dve.wait_ge(S["x2h"], k + 1)
            dve.scalar_tensor_tensor(x2s[1][:, k, :], x1[:, k, :], gain_ffn[:, k:k + 1], high_of(x2s[0][:, k, :]),
                                     ALU.mult, ALU.subtract).then_inc(S["x2l"], 1)
            if k == 3:
                square_low(KB - 1)
        dve.wait_ge(S["sqrt4"], 3)
        link(dve.reciprocal(rstd4[:], rstd4[:]))
        for h in range(2):
            dve.memset(ub[h][:, 0:2], 0.0).then_inc(S["pads"], 1)
            dve.memset(ct[h][:, 0:2], 0.0).then_inc(S["pads"], 1)
        dve.sem_inc(S["u_free"], 2)
        dve.sem_inc(S["gl_free"], 1)
        blk, f0 = 2 * KB, 0
        for gi, ng in enumerate(GROUPS):
            with dve.Fori(0, ng) as i:
                for h in range(2):
                    dve.wait_ge(S["u_free"], i * 2 + (2 * f0 + h + 1))
                    for c, (c0, m) in enumerate(CHUNKS):
                        x = 3 * h + c
                        dve.wait_ge(S["up_f"], i * 6 + (6 * f0 + x + 1))
                        src = ring_u[x]
                        if c < 2:
                            r = dve.tensor_tensor(ub[h][:, c0 + 2:c0 + 2 + m], src[:, 0:m], rstd4[:, c0:c0 + m], ALU.mult)
                        else:
                            dve.tensor_tensor(ub[h][:, c0 + 2:T_P + 2], src[:, 0:T_P - c0], rstd4[:, c0:T_P], ALU.mult)
                            r = dve.tensor_tensor(ub[h][:, T_P + 4:TU], src[:, T_P - c0:m], rstd4[:, T_P:T], ALU.mult)
                        r.then_inc(S["up_free"], 1)
                    b = i + (f0 + FB * h)
                    dve.wait_ge(S["ct_a"], i * 2 + (2 * f0 + h + 1))
                    dve.scalar_tensor_tensor(ct[h][:], ub[h][:, 1:TU - 1], taps[1][:, bass.ds(b, 1)], ct[h][:],
                                             ALU.mult, ALU.add).then_inc(S["c1_d"], 1)
                    gap = TU - 2 - T_P
                    dve.tensor_copy(edges[:, :, b].rearrange("p (a r) -> p a r", r=2),
                                    ub[h][:, T_P:T_P + 2 * gap].rearrange("p (a r) -> p a r", r=gap)[:, :, 0:2]
                                    ).then_inc(S["edge_d"], 1)
                    dve.wait_ge(S["c1_d"], i * 2 + (2 * f0 + h + 1))
                    dve.scalar_tensor_tensor(ct[h][:], ub[h][:, 0:TU - 2], taps[0][:, bass.ds(b, 1)], ct[h][:],
                                             ALU.mult, ALU.add).then_inc(S["u_free"], 1)
                    if h == 0:
                        dve.wait_ge(S["w3h"], i * 2 + (blk + 3))
                        rest(wsp3[0][1][:], wraw3[0][:], wsp3[0][0][:]).then_inc(S["w3l"], 1)
                dve.wait_ge(S["silu_d"], i + (f0 + 1))
                dve.wait_ge(S["u_free"], i * 2 + (2 * f0 + 4))
                dve.tensor_tensor(ct[1][:], ct[0][:], ct[1][:], ALU.mult).then_inc(S["gm_d"], 1)
                dve.wait_ge(S["gh_d"], i + (f0 + 1))
                rest(gsp[1][:, i, 0:T_P], ct[1][:, 0:T_P], gsp[0][:, i, 0:T_P])
                rest(gsp[1][:, i, T_P:T], ct[1][:, T_P + 2:TU - 2], gsp[0][:, i, T_P:T]).then_inc(S["gl_free"], 1)
                dve.wait_ge(S["w3h"], i * 2 + (blk + 4))
                rest(wsp3[1][1][:], wraw3[1][:], wsp3[1][0][:]).then_inc(S["w3l"], 1)
            f0 += ng
            blk += 2 * ng
            final = gi == len(GROUPS) - 1

            def down(i):
                for s in range(2):
                    for c, (c0, m) in enumerate(CHUNKS):
                        x = 3 * s + c
                        dve.wait_ge(S["dn_f"], i * 6 + (24 * gi + x + 1))
                        now = x1[:, i * 2 + s, c0:c0 + m]
                        out = y_blk[s][:, c0:c0 + m] if final else now
                        dve.tensor_tensor(out, ring_d[x % 3][:, 0:m], now, ALU.add).then_inc(S["dn_free"], 1)
                    if not (final and isinstance(i, int)):
                        dve.wait_ge(S["w3h"], i * 2 + (blk + 3 + s))
                        rest(wsp3[s][1][:], wraw3[s][:], wsp3[s][0][:]).then_inc(S["w3l"], 1)

            if final:
                with dve.Fori(0, 3) as i:
                    down(i)
                down(3)
            else:
                with dve.Fori(0, 4) as i:
                    down(i)
            blk += 8

    ctx.close()


_INS = ["x_prompt", "x_sample", "cache_a_k", "cache_a_v", "cache_a_logf", "cache_b_k", "cache_b_v",
        "state_ffn_conv", "g_attn", "w_in", "b_f", "qn_a", "kn_a", "qn_b", "kn_b",
        "lambda_q1", "lambda_k1", "lambda_q2", "lambda_k2", "subln_b", "w_oa", "w_ob", "w_out",
        "g_ffn", "w_up", "conv_w", "conv_b", "w_down"]
_OUTS = [(1, T_P, D), (1, T_S, D),
         (1, T_P, 8, 64), (1, T_P, 8, 64), (1, T_P, 8), (1, T_P, 4, 2, 64), (1, T_P, 4, 128), (1, 2, 2 * D_FF),
         (1, T_S, 8, 64), (1, T_S, 8, 64), (1, T_S, 8), (1, T_S, 4, 2, 64), (1, T_S, 4, 128), (1, 2, 2 * D_FF)]


def kernel(**inputs):
    import numpy as _np
    import concourse.bacc as _bacc
    from concourse import mybir as _mybir
    from concourse.bass_utils import run_bass_kernel_spmd as _run

    nc = _bacc.Bacc("TRN2", target_bir_lowering=False, num_devices=1)
    arrays, ins, outs = {}, [], []
    for name in _INS:
        a = _np.ascontiguousarray(inputs[name])
        arrays[f"in_{name}"] = a
        ins.append(nc.dram_tensor(f"in_{name}", a.shape, _mybir.dt.from_np(a.dtype), kind="ExternalInput").ap())
    for i, shape in enumerate(_OUTS):
        outs.append(nc.dram_tensor(f"out_{i}", shape, _mybir.dt.float32, kind="ExternalOutput").ap())
    build(nc, ins, outs)
    r = _run(nc, [arrays], core_ids=[0])
    return tuple(r.results[0][f"out_{i}"] for i in range(len(_OUTS)))
```
